# Optimizing a Trainium2 kernel written in Bass

```python
import math
import jax
import jax.numpy as jnp
from jax import lax
import numpy as np

D_MODEL = 1024
BATCH = 1
SEQ = 256
DEPTH = 2

GRID_W = 64
CTX_LEN = 256
RMS_EPS = 1e-6
N_BRANCH = 3
BRANCH_W = 512
ATT_HEADS = 8
ATT_KV_HEADS = 2
ATT_HEAD_DIM = 64
ATT_GROUP = ATT_HEADS // ATT_KV_HEADS
Q_BLOCK = 128
ROPE_THETA = 10000.0
SSD_HEADS = 8
SSD_HEAD_DIM = 64
SSD_INNER = SSD_HEADS * SSD_HEAD_DIM
SSD_GROUPS = 2
SSD_STATE = 64
SSD_XBC = SSD_INNER + 2 * SSD_GROUPS * SSD_STATE
SSD_CONV = 5
SSD_CHUNK = 128
ML_HEADS = 4
ML_HEAD_DIM = 128
ML_INNER = ML_HEADS * ML_HEAD_DIM
ML_CHUNK = 128
PEER_HEADS = 8
PEER_KEYS = 128
PEER_EXPERTS = PEER_KEYS * PEER_KEYS
PEER_TOPK = 16
PEER_QDIM = 256
PEER_BLOCK = 128
IN_SPLITS = (ATT_HEADS * ATT_HEAD_DIM, ATT_KV_HEADS * ATT_HEAD_DIM, ATT_KV_HEADS * ATT_HEAD_DIM,
             SSD_INNER, SSD_XBC, 2 * SSD_HEADS,
             ML_INNER, ML_INNER, ML_INNER, ML_INNER, 4 * ML_HEADS,
             N_BRANCH * D_MODEL)
IN_COLS = sum(IN_SPLITS)

kernel_name = 'hybrid_gqa_ssd_mlstm_peer_dit'

def rmsnorm(x, g):
    xf = x.astype(jnp.float32)
    y = xf * lax.rsqrt(jnp.mean(xf * xf, axis=-1, keepdims=True) + RMS_EPS)
    return (y * g.astype(jnp.float32)).astype(x.dtype)

def split_cols(p):
    bounds = np.cumsum(IN_SPLITS)[:-1].tolist()
    return jnp.split(p, bounds, axis=-1)

def heads(t, n):
    return t.reshape(t.shape[0], t.shape[1], n, -1)

def axial_rope(rows):
    n_freq = ATT_HEAD_DIM // 4
    inv = ROPE_THETA ** (-jnp.arange(n_freq, dtype=jnp.float32) / n_freq)
    row = jnp.broadcast_to(jnp.arange(rows, dtype=jnp.float32)[:, None], (rows, GRID_W)).reshape(-1)
    col = jnp.broadcast_to(jnp.arange(GRID_W, dtype=jnp.float32)[None, :], (rows, GRID_W)).reshape(-1)
    ang = jnp.concatenate([row[:, None] * inv, col[:, None] * inv], axis=-1)
    return jnp.cos(ang), jnp.sin(ang)

def apply_rope(t, cos, sin):
    half = t.shape[-1] // 2
    tf = t.astype(jnp.float32)
    t1, t2 = tf[..., :half], tf[..., half:]
    c, s = cos[:, None, :], sin[:, None, :]
    return jnp.concatenate([t1 * c - t2 * s, t1 * s + t2 * c], axis=-1).astype(t.dtype)

def latent_attention(q, k, v, kc, vc):
    Bsz, S = q.shape[0], q.shape[1]
    kk = jnp.concatenate([k, kc], axis=1)
    vv = jnp.concatenate([v, vc], axis=1)
    nb = S // Q_BLOCK
    qb = q.reshape(Bsz, nb, Q_BLOCK, ATT_KV_HEADS, ATT_GROUP, ATT_HEAD_DIM).transpose(1, 0, 2, 3, 4, 5)
    scale = ATT_HEAD_DIM ** -0.5

    def block(qblk):
        s = jnp.einsum('bqkgd,bmkd->bkgqm', qblk, kk).astype(jnp.float32) * scale
        p = jax.nn.softmax(s, axis=-1).astype(vv.dtype)
        return jnp.einsum('bkgqm,bmkd->bqkgd', p, vv)

    o = lax.map(block, qb)
    return o.transpose(1, 0, 2, 3, 4, 5).reshape(Bsz, S, ATT_HEADS * ATT_HEAD_DIM)

def context_attention(qc, kc, vc):
    Bsz, L = qc.shape[0], qc.shape[1]
    qg = qc.reshape(Bsz, L, ATT_KV_HEADS, ATT_GROUP, ATT_HEAD_DIM)
    s = jnp.einsum('blkgd,bmkd->bkglm', qg, kc).astype(jnp.float32) * ATT_HEAD_DIM ** -0.5
    p = jax.nn.softmax(s, axis=-1).astype(vc.dtype)
    o = jnp.einsum('bkglm,bmkd->blkgd', p, vc)
    return o.reshape(Bsz, L, ATT_HEADS * ATT_HEAD_DIM)

def dwconv(x, w, b):
    out = lax.conv_general_dilated(x, w[:, None, :], window_strides=(1,), padding='SAME',
                                   dimension_numbers=('NWC', 'WIO', 'NWC'),
                                   feature_group_count=x.shape[-1])
    return out + b

def segsum(a):
    T = a.shape[-1]
    xa = jnp.broadcast_to(a[..., None], a.shape + (T,))
    xa = jnp.where(jnp.tril(jnp.ones((T, T), bool), -1), xa, 0.0)
    cs = jnp.cumsum(xa, axis=-2)
    return jnp.where(jnp.tril(jnp.ones((T, T), bool)), cs, -jnp.inf)

def ssd_scan(x, dt, A, Bm, Cm, init, with_output):
    Bsz, T, H, P = x.shape
    G, N = Bm.shape[2], Bm.shape[3]
    R = H // G
    Q = SSD_CHUNK
    nc = T // Q
    a = dt * A
    xc = (x * dt[..., None]).reshape(Bsz, nc, Q, G, R, P)
    ac = a.reshape(Bsz, nc, Q, G, R).transpose(0, 3, 4, 1, 2)
    Bc = Bm.reshape(Bsz, nc, Q, G, N)
    Cc = Cm.reshape(Bsz, nc, Q, G, N)
    a_cum = jnp.cumsum(ac, axis=-1)
    decay_states = jnp.exp(a_cum[..., -1:] - a_cum)
    states = jnp.einsum('bcqgn,bgrcq,bcqgrp->bcgrpn', Bc, decay_states, xc)
    init_c = init.reshape(Bsz, G, R, P, N)[:, None]
    states = jnp.concatenate([init_c, states.astype(init_c.dtype)], axis=1)
    chunk_decay = jnp.exp(segsum(jnp.pad(a_cum[..., -1], [(0, 0)] * 3 + [(1, 0)])))
    new_states = jnp.einsum('bgrzc,bcgrpn->bzgrpn', chunk_decay, states)
    start_states = new_states[:, :-1]
    final = new_states[:, -1].reshape(Bsz, H, P, N)
    if not with_output:
        return None, final
    Lmat = jnp.exp(segsum(ac))
    y_diag = jnp.einsum('bcqgn,bcsgn,bgrcqs,bcsgrp->bcqgrp', Cc, Bc, Lmat, xc)
    y_off = jnp.einsum('bcqgn,bcgrpn,bgrcq->bcqgrp', Cc, start_states, jnp.exp(a_cum))
    return (y_diag + y_off).reshape(Bsz, T, H, P), final

def ssd_zero_state(Bsz):
    z = jnp.zeros((Bsz, SSD_HEADS, SSD_HEAD_DIM, SSD_STATE), jnp.float32)
    return (z, z)

def ssd_mixer(z, xbc, dt_raw, conv_w, conv_b, dt_bias, a_log, d_skip, norm_g, inits, with_output):
    Bsz, T, _ = xbc.shape
    xbc = jax.nn.silu(dwconv(xbc, conv_w, conv_b))
    xs, Bm, Cm = jnp.split(xbc, [SSD_INNER, SSD_INNER + SSD_GROUPS * SSD_STATE], axis=-1)
    xs = xs.reshape(Bsz, T, SSD_HEADS, SSD_HEAD_DIM)
    Bm = Bm.reshape(Bsz, T, SSD_GROUPS, SSD_STATE)
    Cm = Cm.reshape(Bsz, T, SSD_GROUPS, SSD_STATE)
    dt = jax.nn.softplus(dt_raw.reshape(Bsz, T, 2, SSD_HEADS).astype(jnp.float32) + dt_bias.astype(jnp.float32))
    A = -jnp.exp(a_log.astype(jnp.float32))
    fl = lambda t: jnp.flip(t, axis=1)
    y_f, fin_f = ssd_scan(xs, dt[:, :, 0], A[0], Bm, Cm, inits[0], with_output)
    y_b, fin_b = ssd_scan(fl(xs), fl(dt[:, :, 1]), A[1], fl(Bm), fl(Cm), inits[1], with_output)
    if not with_output:
        return None, (fin_f, fin_b)
    y = y_f + fl(y_b) + xs.astype(jnp.float32) * d_skip.astype(jnp.float32)[:, None]
    y = y.reshape(Bsz, T, SSD_INNER).astype(z.dtype) * jax.nn.silu(z)
    return rmsnorm(y, norm_g), (fin_f, fin_b)

def mlstm_scan(q, k, v, i_pre, logf, init, with_output):
    Bsz, T, H, Dh = q.shape
    Q = ML_CHUNK
    nc = T // Q
    qc = q.reshape(Bsz, nc, Q, H, Dh)
    kc = k.reshape(Bsz, nc, Q, H, Dh)
    vc = v.reshape(Bsz, nc, Q, H, Dh)
    ic = i_pre.reshape(Bsz, nc, Q, H).transpose(0, 3, 1, 2)
    b = jnp.cumsum(logf.reshape(Bsz, nc, Q, H).transpose(0, 3, 1, 2), axis=-1)
    b_last = b[..., -1]
    g = b_last[..., None] - b + ic
    m_loc = jnp.max(g, axis=-1)
    w = jnp.exp(g - m_loc[..., None])
    C_loc = jnp.einsum('bhcs,bcshd,bcshe->bchde', w, vc, kc)
    n_loc = jnp.einsum('bhcs,bcshe->bche', w, kc)

    def step(carry, inp):
        C, n, m = carry
        Cl, nl, ml, bl = inp
        m_new = jnp.maximum(bl + m, ml)
        a_prev = jnp.exp(bl + m - m_new)
        a_loc = jnp.exp(ml - m_new)
        C_new = a_prev[..., None, None] * C + a_loc[..., None, None] * Cl
        n_new = a_prev[..., None] * n + a_loc[..., None] * nl
        return (C_new, n_new, m_new), (C, n, m)

    xs = (C_loc.transpose(1, 0, 2, 3, 4), n_loc.transpose(1, 0, 2, 3),
          m_loc.transpose(2, 0, 1), b_last.transpose(2, 0, 1))
    final, (C0, n0, m0) = lax.scan(step, init, xs)
    if not with_output:
        return None, final
    m0 = m0.transpose(1, 2, 0)
    Dm = b[..., :, None] - b[..., None, :] + ic[..., None, :]
    Dm = jnp.where(jnp.tril(jnp.ones((Q, Q), bool)), Dm, -jnp.inf)
    inter = b + m0[..., None]
    m_t = jnp.maximum(inter, jnp.max(Dm, axis=-1))
    Wts = jnp.exp(Dm - m_t[..., None])
    w_inter = jnp.exp(inter - m_t)
    s = jnp.einsum('bcqhd,bcshd->bhcqs', qc, kc) * Wts
    num = (jnp.einsum('bhcqs,bcshd->bcqhd', s, vc)
           + jnp.einsum('bcqhe,cbhde->bcqhd', qc, C0) * w_inter.transpose(0, 2, 3, 1)[..., None])
    den = jnp.sum(s, axis=-1) + w_inter * jnp.einsum('bcqhe,cbhe->bhcq', qc, n0)
    denom = jnp.maximum(jnp.abs(den), jnp.exp(-m_t)).transpose(0, 2, 3, 1)[..., None]
    return (num / denom).reshape(Bsz, T, H, Dh), final

def mlstm_zero_state(Bsz):
    st = (jnp.zeros((Bsz, ML_HEADS, ML_HEAD_DIM, ML_HEAD_DIM), jnp.float32),
          jnp.zeros((Bsz, ML_HEADS, ML_HEAD_DIM), jnp.float32),
          jnp.zeros((Bsz, ML_HEADS), jnp.float32))
    return (st, st)

def mlstm_mixer(q, k, v, o_pre, if_pre, gate_bias, norm_g, inits, with_output):
    Bsz, T, _ = q.shape
    out_dtype = q.dtype
    qh = heads(q, ML_HEADS).astype(jnp.float32)
    kh = heads(k, ML_HEADS).astype(jnp.float32) * ML_HEAD_DIM ** -0.5
    vh = heads(v, ML_HEADS).astype(jnp.float32)
    gates = if_pre.reshape(Bsz, T, 2, 2, ML_HEADS).astype(jnp.float32) + gate_bias.astype(jnp.float32)
    i_pre = gates[:, :, :, 0]
    logf = jax.nn.log_sigmoid(gates[:, :, :, 1])
    fl = lambda t: jnp.flip(t, axis=1)
    h_f, fin_f = mlstm_scan(qh, kh, vh, i_pre[:, :, 0], logf[:, :, 0], inits[0], with_output)
    h_b, fin_b = mlstm_scan(fl(qh), fl(kh), fl(vh), fl(i_pre[:, :, 1]), fl(logf[:, :, 1]), inits[1], with_output)
    if not with_output:
        return None, (fin_f, fin_b)
    h = rmsnorm(h_f + fl(h_b), norm_g).reshape(Bsz, T, ML_INNER)
    h = h * jax.nn.sigmoid(o_pre.astype(jnp.float32))
    return h.astype(out_dtype), (fin_f, fin_b)

def merge_branches(branches, gate_pre, w_branch, w_out):
    Bsz, T, _ = gate_pre.shape
    stacked = jnp.stack(branches, axis=2)
    proj = jnp.einsum('btrw,rwd->btrd', stacked, w_branch)
    gates = jax.nn.sigmoid(gate_pre.reshape(Bsz, T, N_BRANCH, D_MODEL))
    return jnp.sum(gates * proj, axis=2) @ w_out

def token_mixer(h, hc, w_in, qn, kn, conv_w, conv_b, dt_bias, a_log, d_skip, ssd_norm_g,
                ml_bias, ml_norm_g, w_branch, w_out, cos, sin, ctx_out):
    Bsz = h.shape[0]
    aq, ak, av, sz, sxbc, sdt, mq, mk, mv, mo, mif, gpre = split_cols(h @ w_in)
    caq, cak, cav, csz, csxbc, csdt, cmq, cmk, cmv, cmo, cmif, cgpre = split_cols(hc @ w_in)
    q = apply_rope(rmsnorm(heads(aq, ATT_HEADS), qn), cos, sin)
    k = apply_rope(rmsnorm(heads(ak, ATT_KV_HEADS), kn), cos, sin)
    kc = rmsnorm(heads(cak, ATT_KV_HEADS), kn)
    vc = heads(cav, ATT_KV_HEADS)
    att = latent_attention(q, k, heads(av, ATT_KV_HEADS), kc, vc)
    ssd_c, ssd_fin = ssd_mixer(csz, csxbc, csdt, conv_w, conv_b, dt_bias, a_log, d_skip, ssd_norm_g,
                               ssd_zero_state(Bsz), ctx_out)
    ssd_l, _ = ssd_mixer(sz, sxbc, sdt, conv_w, conv_b, dt_bias, a_log, d_skip, ssd_norm_g, ssd_fin, True)
    ml_c, ml_fin = mlstm_mixer(cmq, cmk, cmv, cmo, cmif, ml_bias, ml_norm_g, mlstm_zero_state(Bsz), ctx_out)
    ml_l, _ = mlstm_mixer(mq, mk, mv, mo, mif, ml_bias, ml_norm_g, ml_fin, True)
    y = merge_branches((att, ssd_l, ml_l), gpre, w_branch, w_out)
    if not ctx_out:
        return y, None
    att_c = context_attention(rmsnorm(heads(caq, ATT_HEADS), qn), kc, vc)
    yc = merge_branches((att_c, ssd_c, ml_c), cgpre, w_branch, w_out)
    return y, yc

def peer(h, w_q, subkeys, u, v):
    n_tok = h.shape[0]
    hb = h.reshape(n_tok // PEER_BLOCK, PEER_BLOCK, D_MODEL)

    def block(xb):
        q = (xb @ w_q).reshape(PEER_BLOCK, PEER_HEADS, 2, PEER_QDIM // 2)
        s = jnp.einsum('thpd,hpkd->thpk', q, subkeys).astype(jnp.float32)
        s1, i1 = lax.top_k(s[:, :, 0], PEER_TOPK)
        s2, i2 = lax.top_k(s[:, :, 1], PEER_TOPK)
        cand = (s1[..., :, None] + s2[..., None, :]).reshape(PEER_BLOCK, PEER_HEADS, PEER_TOPK * PEER_TOPK)
        cidx = (i1[..., :, None] * PEER_KEYS + i2[..., None, :]).reshape(PEER_BLOCK, PEER_HEADS, PEER_TOPK * PEER_TOPK)
        sc, pos = lax.top_k(cand, PEER_TOPK)
        idx = jnp.take_along_axis(cidx, pos, axis=-1)
        g = jax.nn.softmax(sc, axis=-1).astype(xb.dtype)
        act = jax.nn.gelu(jnp.einsum('thkd,td->thk', u[idx], xb))
        return jnp.einsum('thk,thkd->td', g * act, v[idx])

    return lax.map(block, hb).reshape(n_tok, D_MODEL)

def setup_inputs(seed: int = 0) -> dict:
    key = jax.random.key(seed)
    ks = jax.random.split(key, 28)
    f32 = jnp.float32
    L = DEPTH

    def nrm(k, shape, s):
        return jax.random.normal(k, shape, f32) * s

    dt0 = jnp.exp(jax.random.uniform(ks[12], (L, 2, SSD_HEADS), f32, math.log(1e-3), math.log(1e-1)))
    fgate = jnp.broadcast_to(jnp.linspace(3.0, 6.0, ML_HEADS, dtype=f32), (L, 2, ML_HEADS))
    return {
        'x': nrm(ks[0], (BATCH, SEQ, D_MODEL), 1.0),
        'c': nrm(ks[1], (BATCH, D_MODEL), 1.0),
        'ctx': nrm(ks[2], (BATCH, CTX_LEN, D_MODEL), 1.0),
        'c_ctx': nrm(ks[3], (D_MODEL,), 1.0),
        'norm1_g': 1.0 + nrm(ks[4], (L, D_MODEL), 0.02),
        'norm2_g': 1.0 + nrm(ks[5], (L, D_MODEL), 0.02),
        'w_mod': nrm(ks[6], (L, D_MODEL, 6 * D_MODEL), 0.02),
        'b_mod': nrm(ks[7], (L, 6 * D_MODEL), 0.01),
        'w_in': nrm(ks[8], (L, D_MODEL, IN_COLS), D_MODEL ** -0.5),
        'att_qnorm': 1.0 + nrm(ks[9], (L, ATT_HEAD_DIM), 0.02),
        'att_knorm': 1.0 + nrm(ks[10], (L, ATT_HEAD_DIM), 0.02),
        'ssd_conv_w': nrm(ks[11], (L, SSD_CONV, SSD_XBC), SSD_CONV ** -0.5),
        'ssd_conv_b': nrm(ks[13], (L, SSD_XBC), 0.01),
        'ssd_dt_bias': dt0 + jnp.log(-jnp.expm1(-dt0)),
        'ssd_a_log': jnp.log(jax.random.uniform(ks[14], (L, 2, SSD_HEADS), f32, 1.0, 16.0)),
        'ssd_d': 1.0 + nrm(ks[15], (L, SSD_HEADS), 0.1),
        'ssd_norm': 1.0 + nrm(ks[16], (L, SSD_INNER), 0.02),
        'ml_gate_bias': jnp.stack([nrm(ks[17], (L, 2, ML_HEADS), 0.1),
                                   fgate + nrm(ks[18], (L, 2, ML_HEADS), 0.1)], axis=2),
        'ml_norm': 1.0 + nrm(ks[19], (L, ML_HEADS, ML_HEAD_DIM), 0.02),
        'w_branch': nrm(ks[20], (L, N_BRANCH, BRANCH_W, D_MODEL), BRANCH_W ** -0.5),
        'w_out': nrm(ks[21], (L, D_MODEL, D_MODEL), D_MODEL ** -0.5),
        'peer_wq': nrm(ks[22], (L, D_MODEL, PEER_HEADS * PEER_QDIM), D_MODEL ** -0.5),
        'peer_subkeys': nrm(ks[23], (L, PEER_HEADS, 2, PEER_KEYS, PEER_QDIM // 2), (PEER_QDIM // 2) ** -0.5),
        'peer_u': nrm(ks[24], (L, PEER_EXPERTS, D_MODEL), D_MODEL ** -0.5),
        'peer_v': nrm(ks[25], (L, PEER_EXPERTS, D_MODEL), PEER_HEADS ** -0.5),
    }

def reference(x, c, ctx, c_ctx, norm1_g, norm2_g, w_mod, b_mod, w_in, att_qnorm, att_knorm,
              ssd_conv_w, ssd_conv_b, ssd_dt_bias, ssd_a_log, ssd_d, ssd_norm, ml_gate_bias, ml_norm,
              w_branch, w_out, peer_wq, peer_subkeys, peer_u, peer_v):
    Bsz, S, _ = x.shape
    ROWS = S // GRID_W
    cos, sin = axial_rope(ROWS)
    silu_c = jax.nn.silu(c)
    silu_cc = jax.nn.silu(c_ctx)
    xc = ctx
    for l in range(DEPTH):
        last = l == DEPTH - 1
        sh1, sc1, g1, sh2, sc2, g2 = jnp.split((silu_c @ w_mod[l] + b_mod[l])[:, None, :], 6, axis=-1)
        csh1, csc1, cg1, csh2, csc2, cg2 = jnp.split(silu_cc @ w_mod[l] + b_mod[l], 6, axis=-1)
        h = rmsnorm(x, norm1_g[l]) * (1.0 + sc1) + sh1
        hc = rmsnorm(xc, norm1_g[l]) * (1.0 + csc1) + csh1
        y, yc = token_mixer(h, hc, w_in[l], att_qnorm[l], att_knorm[l], ssd_conv_w[l], ssd_conv_b[l],
                            ssd_dt_bias[l], ssd_a_log[l], ssd_d[l], ssd_norm[l], ml_gate_bias[l], ml_norm[l],
                            w_branch[l], w_out[l], cos, sin, not last)
        x = x + g1 * y
        h2 = rmsnorm(x, norm2_g[l]) * (1.0 + sc2) + sh2
        x = x + g2 * peer(h2.reshape(-1, D_MODEL), peer_wq[l], peer_subkeys[l], peer_u[l], peer_v[l]).reshape(x.shape)
        if not last:
            xc = xc + cg1 * yc
            hc2 = rmsnorm(xc, norm2_g[l]) * (1.0 + csc2) + csh2
            xc = xc + cg2 * peer(hc2.reshape(-1, D_MODEL), peer_wq[l], peer_subkeys[l], peer_u[l], peer_v[l]).reshape(xc.shape)
    return x


_drawn_inputs = setup_inputs


def setup_inputs(seed=0):
    import zlib

    import numpy as np

    out = dict(_drawn_inputs(seed))
    spreads = {}
    factors = {'norm1_g': 3.241,
     'norm2_g': 3.264,
     'b_mod': 2.712,
     'att_qnorm': 8.0,
     'att_knorm': 8.0,
     'ssd_conv_b': 6.526,
     'ssd_d': 15.522,
     'ssd_norm': 5.156,
     'ml_norm': 6.959}
    for name, (base, spread) in spreads.items():
        noise = np.random.default_rng([zlib.crc32(name.encode()), seed]).standard_normal(out[name].shape)
        drawn = base * np.exp(spread * noise) if base else spread * noise
        out[name] = jnp.asarray(drawn.astype(out[name].dtype))
    for name, factor in factors.items():
        out[name] = (out[name] * factor).astype(out[name].dtype)
    return out
```

```python
from contextlib import ExitStack

import numpy as np
import concourse.bass as bass
from concourse import mybir

F32 = mybir.dt.float32
U32 = mybir.dt.uint32
F32R = mybir.dt.float32r
ACT = mybir.ActivationFunctionType
ALU = mybir.AluOpType
AX = mybir.AxisListType

P = 128
D = 1024
KB = D // P
SEQ = 256
T = 512
NT = T // P
DEPTH = 2
EPS = 1e-6
NEG = -1e30

AH, AD = 8, 64
SH, SD, SN = 8, 64, 64
MH, MD = 4, 128
TAPS = 5
PH, TOPK, KEYS = 8, 16, 128

SLOTS = 4
SLOT = 2048
MOD_SLOTS, IN_SLOTS, OUT_SLOTS, WQ_SLOTS = 24, 28, 4, 8
CHUNKS = 128

IN_K, IN_V, IN_B, IN_C, IN_XS, IN_Q, IN_MK, IN_MQ = 0, 1, 2, 3, 4, 8, 12, 16
SLOT_Z, SLOT_MV, SLOT_MO, SLOT_GATE = 10, 12, 14, 16

C_ID, C_U, C_L, C_NMU, C_NML, C_ONE, C_BLK, C_SWAP, C_IOTA, C_COS, C_SIN = (
    0, 128, 256, 384, 512, 640, 768, 896, 1024, 1152, 1408)
C_ALL = 1664

V_N1, V_N2, V_BMOD, V_CW, V_CB, V_SSDN, V_MLN, V_QN, V_KN, V_BIAS, V_ALOG, V_D = (
    0, 8, 16, 64, 94, 100, 104, 108, 109, 110, 142, 158)
V_ALL = 166


def shape_constants():
    k = np.arange(P)
    c = np.zeros((P, C_ALL), np.float32)
    c[:, C_ID:C_ID + P] = np.eye(P)
    upper = k[:, None] <= k[None, :]
    c[:, C_U:C_U + P] = upper
    c[:, C_L:C_L + P] = upper.T
    c[:, C_NMU:C_NMU + P] = np.where(upper, 0.0, NEG)
    c[:, C_NML:C_NML + P] = np.where(upper.T, 0.0, NEG)
    c[:, C_ONE:C_ONE + P] = 1.0
    c[:, C_BLK:C_BLK + P] = (k[:, None] // AD) == (k[None, :] // AD)
    c[:, C_SWAP:C_SWAP + P] = k[:, None] == (k[None, :] ^ 32)
    c[:, C_IOTA:C_IOTA + P] = k[None, :]
    nf = AD // 4
    inv = (np.float32(10000.0) ** (-np.arange(nf, dtype=np.float32) / np.float32(nf))).astype(np.float32)
    tok = np.arange(SEQ)
    row, col = (tok // 64).astype(np.float32), (tok % 64).astype(np.float32)
    ang = np.concatenate([row[:, None] * inv, col[:, None] * inv], axis=-1).astype(np.float32)
    f = k % 32
    c[:, C_COS:C_COS + SEQ] = np.cos(ang)[:, f].T
    c[:, C_SIN:C_SIN + SEQ] = np.sin(ang)[:, f].T * np.where((k % 64) < 32, -1.0, 1.0)[:, None]
    return c


class Counts:

    def __init__(self, known):
        self.known = known
        self.now = {}
        self.sems = {}
        self.count = {}
        self.banks = {}

    def open(self, nc, ctx):
        self.nc, self.ctx = nc, ctx

    def sem(self, topic):
        if topic not in self.sems:
            self.sems[topic] = self.ctx.enter_context(self.nc.semaphore(topic))
        return self.sems[topic]

    def inc(self, topic, *key, by=1):
        self.count[topic] = self.count.get(topic, 0) + by
        self.now[topic, key] = self.count[topic]
        return self.sem(topic), by

    def at(self, topic, *key):
        return self.sem(topic), self.known.get((topic, key), 1)

    def bank(self, topic, *key):
        return self.known.get(("bank", topic, key), 0)


def write_program(nc, x_in, c_in, wmod_in, win_in, wsm_in, wbr_in, wout_in, wq_in, sub_in, u_in, v_in,
                  vec_in, const_in, out, known, upto=99, limit=10**6):
    cnt = Counts(known)
    inc, at = cnt.inc, cnt.at
    with ExitStack() as ctx:
        cnt.open(nc, ctx)

        def sb(name, shape, dt=F32):
            return ctx.enter_context(nc.sbuf_tensor(name, shape, dt))

        ps = [ctx.enter_context(nc.psum_tensor(f"ps{b}", [P, 512], F32)) for b in range(8)]
        XT = sb("XT", [P, KB, T])
        ring_at = nc.sbuf_base
        ring = sb("ring", [P, SLOTS, SLOT])
        const = sb("const", [P, C_ALL])
        vec = sb("vec", [P, DEPTH, V_ALL])
        wsm = sb("wsm", [P, DEPTH, KB, 32])
        csil = sb("csil", [P, KB, 2])
        mod = sb("mod", [P, DEPTH, 48, 2])
        scale1 = sb("scale1", [P, KB, 2])
        scale2 = sb("scale2", [P, KB, 2])
        G_F = CHUNKS * SEQ
        TAIL_F = 5376
        arena_at = nc.sbuf_base
        arena = sb("arena", [P, G_F + TAIL_F])

        cursor = [0]

        def take(*shape):
            n = int(np.prod(shape))
            v = view(cursor[0], *shape)
            cursor[0] += n
            assert cursor[0] <= G_F + TAIL_F, cursor[0]
            return v

        def view(at_, *shape):
            n = int(np.prod(shape))
            v = arena[:, at_:at_ + n]
            if len(shape) == 2:
                v = v.rearrange("p (a b) -> p a b", b=shape[1])
            elif len(shape) == 3:
                v = v.rearrange("p (a b c) -> p a b c", b=shape[1], c=shape[2])
            elif len(shape) == 4:
                v = v.rearrange("p (a b c d) -> p a b c d", b=shape[1], c=shape[2], d=shape[3])
            return v

        hT = take(KB, T)
        merge_at = cursor[0]
        xs_tm = take(NT, 512)
        scr_at = cursor[0]
        qT = take(4, T)
        XPAD = SEQ + TAPS - 1
        xin = take(6, 2, XPAD)
        scr_end = cursor[0]
        mergedT = view(merge_at, KB, T)
        kT = take(T)
        v_tm = take(NT, P)
        xcv = take(6, T)
        B_tm = take(NT, P)
        gs_at = cursor[0]
        mqT = take(MH, T)
        mkT = take(MH, T)
        gsig = view(gs_at, 6, T)
        mk_tm = take(NT, 512)
        mv = take(NT, MH, MD + 1)
        mo = take(NT, 512)
        z = take(NT, 512)
        acc = take(NT, 512)
        s_attT = cursor[0]
        attT = take(4, T)
        s_ssdT = cursor[0]
        ssdT = take(4, T)
        mlT = take(4, T)
        NG = 24
        sm = take(NT, 32)
        ab = take(NT, 32)
        lnp = take(NT, 32)
        dt = take(NT, 16)
        dec = take(NT, NG)
        cums = take(3, NT, NG)
        cm = take(NT, NG)
        ecm = take(NT, 16)
        dw = take(NT, 16)
        etot = take(NT, 16)
        negA = take(16)
        rr = take(NT, 8)
        sml = take(2, 16, 4)
        rsum = take(NT, 8)
        rinv = take(NT, 8)
        mx = take(NT, 8)
        rstd = view(s_attT, T)
        qk_sq = view(s_attT + 512, T)
        qk_raw = view(s_attT + 1024, T)
        qk_rs = view(s_attT + 1536, T)
        qk_n = view(s_attT + 4096, T)
        qk_t = view(s_attT + 4608, T)
        att_p = view(s_ssdT, 2, T)
        att_pT = view(s_ssdT + 1024, 2, 4, P)
        s = scr_at
        xc, xd, dmat, mmat, cb = (view(s, 512), view(s + 512, 512), view(s + 1024, 512),
                                  view(s + 1536, 512), view(s + 2048, 256))
        st, yo = view(s + 2304, 2, 256), view(s + 2816, 512)
        kw, rD, rW, rWT, numt = (view(s, 512), view(s + 512, 512), view(s + 1024, 512),
                                 view(s + 1536, 512), view(s + 2048, MH, MD + 1))
        cst = view(s + 2564, 2, MH, MD + 1)
        inter = view(s + 3596, MH, MD + 1)
        assert s + 3596 + 516 <= scr_end
        scr_end -= 6 * 2 * XPAD
        scr_end = max(scr_end, merge_at + KB * T)

        def rounded(name, at_, *shape):
            return nc.alloc_sbuf_tensor_at(name, [P, *shape], F32R, offset=arena_at + 4 * at_)

        br_high = rounded("br_high", scr_end, 3, 4 * T)
        x_high = rounded("x_high", gs_at + 6 * T, KB, T)
        w_high = rounded("w_high", gs_at + 14 * T, 3, SLOT)
        h2q_high = rounded("h2q_high", gs_at + 6 * T, KB, SEQ)
        h2q_low = rounded("h2q_low", gs_at + 10 * T, KB, SEQ)
        h_low = rounded("h_low", 0, KB, T)
        merged_low = rounded("merged_low", merge_at, KB, T)
        br_low = [rounded(f"br_low{r_}", s_attT + r_ * 4 * T, 4, T) for r_ in range(3)]
        ring_low = nc.alloc_sbuf_tensor_at("ring_low", [P, SLOTS, SLOT], F32R, offset=ring_at)
        assert scr_end + 12 * T <= gs_at and gs_at + 14 * T + 3 * SLOT <= s_attT

        G = view(0, CHUNKS, SEQ)
        qpT = view(0, 16, SEQ)
        scs = [view(4096, 16, KEYS), view(14592, 16, KEYS)]
        modrow = view(17000, 2, 256)
        cand = view(6144, PH, TOPK * TOPK)
        eqm = view(8192, P, TOPK)
        prod = view(10240, P, TOPK)
        v16 = view(12288, 16, TOPK)
        i16 = view(12544, 16, TOPK)
        i16f = view(12800, 16, TOPK)
        sc16 = view(13056, PH, TOPK)
        pos = view(13184, PH, TOPK)
        pa = view(13312, PH, TOPK)
        pb = view(13440, PH, TOPK)
        paf = view(13568, PH, TOPK)
        pbf = view(13696, PH, TOPK)
        sel = view(13824, 3, P)
        g8 = view(14208, 8)
        rstd2 = view(14336, SEQ)
        h2T = view(G_F, KB, SEQ)
        RT = view(G_F + 2048, 3, SEQ)
        hot = view(G_F + 2816, 2, 2, 4, P)
        HALF = D // 2
        raw = ring.rearrange("p a b -> p (a b)")[:, 0:4 * D].rearrange("p (a b) -> p a b", b=D)
        halves = nc.alloc_sbuf_tensor_at("halves", [P, 4, 2, HALF], F32R, offset=ring_at + 4 * 4 * D)
        h2lo = nc.alloc_sbuf_tensor_at("h2lo", [P, KB, SEQ], F32R, offset=arena_at + 4 * G_F)
        h2hi = nc.alloc_sbuf_tensor_at("h2hi", [P, KB, SEQ], F32R, offset=arena_at + 4 * (G_F + 2048))
        ge = view(G_F + 4096, SEQ)
        wt = nc.alloc_sbuf_tensor_at("wt", [P, 2, 2, SEQ], F32R, offset=arena_at + 4 * (G_F + 4352))
        ident = const[:, C_ID:C_ID + P]
        ones = const[:, C_ONE:C_ONE + P]
        iota = const[:, C_IOTA:C_IOTA + P]
        tri = [const[:, C_U:C_U + P], const[:, C_L:C_L + P]]
        nmask = [const[:, C_NMU:C_NMU + P], const[:, C_NML:C_NML + P]]

        layers = range(DEPTH)

        def outs(l):
            return list(range(NT)) if l < DEPTH - 1 else [2, 3]

        def cols(l):
            return 0 if l < DEPTH - 1 else SEQ

        def passes(l):
            return [(l, 0), (l, 1)] if l < DEPTH - 1 else [(l, 1)]

        def passes_before(pp):
            return [q for l in layers for q in passes(l)].index(pp)

        ORDER = [[0, 1, 2, 3], [1, 0, 3, 2]]

        items, start, fences = [], {}, {}
        MOD_AHEAD = (0, 1)

        def item(kind, l, src, width, *last):
            start.setdefault((kind, l), len(items))
            items.append((src, width, last))

        for l in layers:
            if l == 0:
                for n in range(MOD_SLOTS):
                    item("mod", l, wmod_in[l, n], SLOT, "mod_row", l, n)
            t_out = outs(l)[-2]
            last = [("v", l)] + [("conv_in", l, j) for j in (5, 1, 3)]
            last += [("fm", l, ("q", j)) for j in (1, 3)]
            last += [("fm", l, ("mk", j)) for j in (1, 3)]
            last += [("fm", l, ("mq", j)) for j in (1, 3)]
            last += [("z", l, n, t_out) for n in range(2)] + [("mv", l, n, 2) for n in range(2)]
            last += [("mo", l, n, t_out) for n in range(2)]
            for n in range(SLOT_GATE):
                item("in", l, win_in[l, n], SLOT, *last[n])
            for pr in range(4):
                for n in range(3):
                    item("gate", l, win_in[l, SLOT_GATE + 3 * pr + n], SLOT, "gate", l, pr, 2 * n + 1)
                for n in range(2):
                    item("gate", l, wbr_in[l, 2 * pr + n], 1536, "proj", l, 2 * pr + n, 2)
            for n in range(OUT_SLOTS):
                item("out", l, wout_in[l, n], SLOT, "mix", l, 2 * n + 1)
            for pp in passes(l):
                for n in range(WQ_SLOTS):
                    item("wq", pp, wq_in[l, n], SLOT, "pq", pp, 2 * n + 1)
                item("sub", pp, sub_in[l], SLOT, "psc", pp, 1, 3)
                if pp == MOD_AHEAD:
                    for n in range(MOD_SLOTS):
                        item("mod", l + 1, wmod_in[l + 1, n], SLOT, "mod_row", l + 1, n)
                fences[len(items)] = pp
        split_items = [start["gate", l] + n for l in layers for n in range(20 + OUT_SLOTS)]
        split_items = sorted(split_items + [start["wq", pp] + n for l in layers for pp in passes(l)
                                            for n in range(WQ_SLOTS)])

        def high_of(n):
            return w_high[:, split_items.index(n) % 3, 0:items[n][1]]

        def low_of(n):
            return ring_low[:, n % SLOTS, 0:items[n][1]]

        def merge_item(l, i):
            return start["gate", l] + i

        ITER = (CHUNKS - 1) // 2
        N_ITEMS = 2 * CHUNKS

        def u_item(c):
            return 2 * c - 1 if c else 0

        def v_item(c):
            return 2 * c + 2 if c < CHUNKS - 1 else N_ITEMS - 1

        block = ctx.enter_context(nc.Block())

        @block.sync
        def _(sp):
            sp.dma_start(const[:, :], const_in).then_inc(*inc("const_in", by=16))
            sp.dma_start(vec[:, :, :], vec_in).then_inc(*inc("vec_in", by=16))
            sp.dma_start(csil[:, :, :], c_in).then_inc(*inc("c_in", by=16))
            sp.dma_start(XT[:, :, :], x_in).then_inc(*inc("x_in", by=16))

            def experts(pp):
                l, p = pp[0], passes_before(pp)
                sp.wait_ge(*at("psc", pp, 1, 3))
                if pp == MOD_AHEAD:
                    sp.wait_ge(*at("mod_row", pp[0] + 1, MOD_SLOTS - 1))

                def chunk(src, i):
                    sp.dma_start(raw[:, i % 4, :], src).then_inc(cnt.sem(f"raw{i % 4}"), 16)

                chunk(u_in[l, 0], 0)
                for i in (1, 2, 3):
                    chunk((v_in, u_in)[i % 2][l, i // 2 + (i % 2) - (1 - i % 2)], i)
                with sp.Fori(1, ITER) as it:
                    for j in range(4):
                        sp.wait_ge(cnt.sem("low_made"), it * 8 + (p * 2 * N_ITEMS + 2 * j - 6))
                        src = (v_in, u_in)[j % 2]
                        c = it * 2 + (j // 2 + (j % 2) - (1 - j % 2))
                        sp.dma_start(raw[:, j, :], src[l, bass.ds(c, 1), :, :].rearrange("a p f -> p (a f)")
                                     ).then_inc(cnt.sem(f"raw{j}"), 16)
                for i in range(4 * ITER, N_ITEMS):
                    sp.wait_ge(cnt.sem("low_made"), p * 2 * N_ITEMS + 2 * i - 6)
                    u_next = i % 2 and i < N_ITEMS - 1
                    chunk(u_in[l, i // 2 + 1] if u_next else v_in[l, i // 2 - 1 + i % 2], i)
                sp.wait_ge(cnt.sem("half_free"), (p + 1) * 2 * N_ITEMS + 4)

            def load(n):
                src, w, _ = items[n]
                if n >= SLOTS:
                    topic, *key = items[n - SLOTS][2]
                    sp.wait_ge(*at(topic, *key))
                sp.dma_start(ring[:, n % SLOTS, 0:w], src).then_inc(cnt.sem(f"slot{n % SLOTS}"), 16)

            for n in range(min(limit, len(items))):
                if n in fences and n:
                    experts(fences[n])
                load(n)
            if limit < 10**6:
                return
            experts(fences[len(items)])
            if limit < 10**6:
                return
            last = passes(DEPTH - 1)[-1]
            sp.wait_ge(*at("x_moe", last))
            sp.dma_start(out, XT[:, :, SEQ:T]).then_inc(*inc("stored", by=16))
            sp.wait_ge(*at("stored"))

        @block.tensor
        def _(pe):
            holder = [None] * 8
            turn = [0]

            pinned = set()

            def claim(topic, *key):
                while turn[0] % 8 in pinned:
                    turn[0] += 1
                b = turn[0] % 8
                turn[0] += 1
                if holder[b]:
                    pe.wait_ge(*at(*holder[b]))
                holder[b] = (topic + "_read", *key)
                cnt.now["bank", topic, key] = b
                return ps[b]

            def slot(n):
                pe.wait_ge(cnt.sem(f"slot{n % SLOTS}"), 16 * (n // SLOTS + 1))
                return ring[:, n % SLOTS, :]

            def mm(o, l_, r, first=True, last=True):
                return pe.matmul(o, l_, r, start=first, stop=last)

            def split_slot(n, k):
                pe.wait_ge(*at("item_low", n))
                return [a.rearrange("p (k m) -> p k m", k=k) for a in (high_of(n), low_of(n))]

            def mm3(o, w, x, first, last):
                mm(o, w[0], x[0], first, False)
                mm(o, w[0], x[1], False, False)
                return mm(o, w[1], x[0], False, last)

            mod_bank = [None]

            def mod_open(l):
                mod_bank[0] = claim("mod", l)
                pinned.add((turn[0] - 1) % 8)

            def mod_rows(l, first, end):
                def turn_row(n):
                    pe.wait_ge(*at("mod_row_read", l, n))
                    for j in range(2):
                        c = 2 * (2 * n + j)
                        i = pe.transpose(mod_bank[0][:, c:c + 2], modrow[0:2, n % 2, j * P:(j + 1) * P], ident[0:2, 0:2])
                    i.then_inc(*inc("mod_turn", l, n))

                for n in range(first, end):
                    w = slot(start["mod", l] + n).rearrange("p (k m) -> p k m", k=KB)
                    b = claim("mod_row", l, n)
                    for k in range(KB):
                        i = mm(b[0:2, 0:256], csil[:, k, :], w[:, k, :], k == 0, k == KB - 1)
                    i.then_inc(*inc("mod_row", l, n))
                    if n > first:
                        turn_row(n - 1)
                turn_row(end - 1)

            pe.wait_ge(*at("const_in"))
            for l in layers:
                if upto < 0:
                    break
                oc, n_out = cols(l), T - cols(l)
                if l == 0:
                    pe.wait_ge(*at("csil"))
                    mod_open(0)
                    mod_rows(0, 0, MOD_SLOTS)
                    pinned.clear()

                b = claim("ss1", l)
                for k in range(KB):
                    pe.wait_ge(*at("sq1", l, k))
                    i = mm(b[:, :], ones, hT[:, k, :], k == 0, k == KB - 1)
                i.then_inc(*inc("ss1", l))

                for k in range(KB):
                    pe.wait_ge(*at("hT", l, k))
                if l == 0:
                    pe.wait_ge(*at("x_in"))
                pe.wait_ge(cnt.sem("wsm_in"), 16 * DEPTH)
                b = claim("small", l)
                for t in range(NT):
                    for k in range(KB):
                        i = mm(b[:, t * 32:t * 32 + 32], hT[:, k, t * P:(t + 1) * P], wsm[:, l % 2, k, :],
                               k == 0, k == KB - 1)
                i.then_inc(*inc("small", l))

                def feature_blocks(n, topic, ids, c0):
                    w = slot(n).rearrange("p (k m) -> p k m", k=KB)
                    for j, key in enumerate(ids):
                        if key is None:
                            continue
                        b = claim(topic, l, key)
                        for k in range(KB):
                            i = mm(b[:, c0:T], w[:, k, j * P:(j + 1) * P], hT[:, k, c0:T], k == 0, k == KB - 1)
                        i.then_inc(*inc(topic, l, key))
                    return w

                s0 = start["in", l]
                w = feature_blocks(s0, "fm", ["k", None], 0)
                b = claim("v", l)
                for t in range(NT):
                    for k in range(KB):
                        i = mm(b[:, t * P:(t + 1) * P], hT[:, k, t * P:(t + 1) * P], w[:, k, P:2 * P],
                               k == 0, k == KB - 1)
                i.then_inc(*inc("v", l))
                feature_blocks(s0 + 1, "conv_in", [4, 5], 0)
                for n in range(2):
                    feature_blocks(s0 + 2 + n, "conv_in", [2 * n, 2 * n + 1], 0)
                def qk_finish(key, c0):
                    b = claim("qk_ss", l, key)
                    pe.wait_ge(*at("qk_sq", l, key))
                    mm(b[:, c0:T], const[:, C_BLK:C_BLK + P], qk_sq[:, c0:T]).then_inc(*inc("qk_ss", l, key))
                    b = claim("qk_swap", l, key)
                    pe.wait_ge(*at("qk_n", l, key))
                    mm(b[:, 0:SEQ], const[:, C_SWAP:C_SWAP + P], qk_n[:, SEQ:T]).then_inc(*inc("qk_swap", l, key))

                qk_finish("k", 0)
                for n in range(2):
                    feature_blocks(s0 + 4 + n, "fm", [("q", 2 * n), ("q", 2 * n + 1)], oc)
                    qk_finish(("q", 2 * n), oc)
                    qk_finish(("q", 2 * n + 1), oc)
                for n in range(2):
                    feature_blocks(s0 + 6 + n, "fm", [("mk", 2 * n), ("mk", 2 * n + 1)], 0)
                for n in range(2):
                    feature_blocks(s0 + 8 + n, "fm", [("mq", 2 * n), ("mq", 2 * n + 1)], oc)

                def token_slots(first, name, tiles):
                    for n in range(2):
                        w = slot(s0 + first + n).rearrange("p (k m) -> p k m", k=KB)
                        for t0 in tiles[::2]:
                            b = claim(name, l, n, t0)
                            for t in (t0, t0 + 1):
                                for k in range(KB):
                                    i = mm(b[:, (t - t0) * 256:(t - t0) * 256 + 256],
                                           hT[:, k, t * P:(t + 1) * P], w[:, k, :], k == 0, k == KB - 1)
                            i.then_inc(*inc(name, l, n, t0))

                token_slots(SLOT_Z, "z", outs(l))
                token_slots(SLOT_MV, "mv", list(range(NT)))
                token_slots(SLOT_MO, "mo", outs(l))

                for t in range(NT):
                    b = claim("mk_t", l, t)
                    pe.wait_ge(*at("fm_read", l, ("mk", 3)))
                    for h in range(MH):
                        i = pe.transpose(b[:, h * P:(h + 1) * P], mkT[:, h, t * P:(t + 1) * P], ident)
                    i.then_inc(*inc("mk_t", l, t))
                pe.wait_ge(*at("conv", l, 3))
                for t in range(NT):
                    b = claim("xs_t", l, t)
                    for j in range(4):
                        i = pe.transpose(b[:, j * P:(j + 1) * P], xcv[:, j, t * P:(t + 1) * P], ident)
                    i.then_inc(*inc("xs_t", l, t))
                b = claim("B_t", l)
                for t in range(NT):
                    i = pe.transpose(b[:, t * P:(t + 1) * P], xcv[:, 4, t * P:(t + 1) * P], ident)
                i.then_inc(*inc("B_t", l))

                b = claim("cums", l)
                pe.wait_ge(*at("decays", "dec", l))
                flat = dec.rearrange("p a b -> p (a b)")
                for n, m in enumerate((tri[0], tri[1], ones)):
                    i = mm(b[:, n * NT * NG:(n + 1) * NT * NG], m, flat)
                i.then_inc(*inc("cums", l))
                if upto < 1:
                    break

                for t in outs(l):
                    keys = T if t >= 2 else SEQ

                    def scores(h):
                        half, j = h // 4, h % 4
                        b = claim("att_s", l, t, h)
                        pe.wait_ge(*at("qk_done", l, ("q", 3)))
                        mm(b[:, 0:keys], qT[half * AD:half * AD + AD, j, t * P:(t + 1) * P],
                           kT[half * AD:half * AD + AD, 0:keys]).then_inc(*inc("att_s", l, t, h))

                    def turn_p(h):
                        b = claim("att_t", l, t, h)
                        pe.wait_ge(*at("att_s_read", l, t, h))
                        for m in range(keys // P):
                            i = pe.transpose(b[:, m * P:(m + 1) * P], att_p[:, h % 2, m * P:(m + 1) * P], ident)
                        i.then_inc(*inc("att_t", l, t, h))

                    scores(0)
                    for h in range(AH):
                        if h + 1 < AH:
                            scores(h + 1)
                        turn_p(h)
                        if h == 0:
                            bo = claim("att_o", l, t)
                            pinned.add((turn[0] - 1) % 8)
                            pe.wait_ge(*at("v_read", l))
                        pe.wait_ge(*at("att_t_read", l, t, h))
                        for m in range(keys // P):
                            i = mm(bo[:, h * AD:(h + 1) * AD], att_pT[:, h % 2, m, :],
                                   v_tm[:, m, (h // 4) * AD:(h // 4) * AD + AD], m == 0, m == keys // P - 1)
                        i.then_inc(*inc("att_pv", l, t, h))
                    pinned.clear()
                    b = claim("att_oT", l, t)
                    pe.wait_ge(*at("att_o_read", l, t))
                    for j in range(4):
                        i = pe.transpose(b[:, j * P:(j + 1) * P], acc[:, t, j * P:(j + 1) * P], ident)
                    i.then_inc(*inc("att_oT", l, t))
                if upto < 2:
                    break

                for d in range(2):
                    for n, t in enumerate(ORDER[d]):
                        tc = slice(t * P, (t + 1) * P)
                        if t in outs(l):
                            for g in range(2):
                                b = claim("ssd_cb", l, d, t, g)
                                gp = slice(g * SN, g * SN + SN)
                                mm(b[:, 0:P], xcv[gp, 4, tc], xcv[gp, 5, tc]).then_inc(*inc("ssd_cb", l, d, t, g))
                            for g in range(2):
                                b = claim("ssd_row", l, d, t, g)
                                pe.wait_ge(*at("decays", "cm", l))
                                for j in range(4):
                                    h = d * 8 + g * 4 + j
                                    i = mm(b[:, j * P:(j + 1) * P], cm[:, t, h:h + 1].broadcast_to([P, P]), ident)
                                i.then_inc(*inc("ssd_row", l, d, t, g))
                            if n:
                                pe.wait_ge(*at("ssd_dst_read", l, d, n - 1))
                                for g in range(2):
                                    b = claim("ssd_off", l, d, t, g)
                                    gp = slice(g * SN, g * SN + SN)
                                    mm(b[:, 0:256], xcv[gp, 5, tc], st[gp, (n - 1) % 2, :]
                                       ).then_inc(*inc("ssd_off", l, d, t, g))
                            b = claim("ssd_y", l, d, t)
                            for g in range(2):
                                pe.wait_ge(*at("ssd_m", l, d, t, g))
                                for j in range(4):
                                    h = g * 4 + j
                                    i = mm(b[:, h * SD:(h + 1) * SD], mmat[:, j * P:(j + 1) * P],
                                           xc[:, h * SD:(h + 1) * SD])
                                i.then_inc(*inc("ssd_mm", l, d, t, g))
                        if n < NT - 1:
                            b = claim("ssd_dst", l, d, n)
                            pe.wait_ge(*at("ssd_xd", l, d, n))
                            pe.wait_ge(*at("B_t_read", l))
                            mm(b[:, :], B_tm[:, t, :], xd[:, :]).then_inc(*inc("ssd_dst", l, d, n))
                for t in outs(l):
                    b = claim("ssd_T", l, t)
                    pe.wait_ge(*at("ssd_norm", l, t))
                    for j in range(4):
                        i = pe.transpose(b[:, j * P:(j + 1) * P], acc[:, t, j * P:(j + 1) * P], ident)
                    i.then_inc(*inc("ssd_T", l, t))
                if upto < 3:
                    break

                for d in range(2):
                    for n, t in enumerate(ORDER[d]):
                        tc = slice(t * P, (t + 1) * P)
                        b = claim("ml_row", l, d, t)
                        pe.wait_ge(*at("decays", "cm", l))
                        for h in range(MH):
                            c = d * MH + h
                            i = mm(b[:, h * P:(h + 1) * P], rr[:, t, c:c + 1].broadcast_to([P, P]), ident)
                        i.then_inc(*inc("ml_row", l, d, t))
                        if t in outs(l):
                            b = claim("ml_qk", l, d, t)
                            for h in range(MH):
                                i = mm(b[:, h * P:(h + 1) * P], mqT[:, h, tc], mkT[:, h, tc])
                            i.then_inc(*inc("ml_qk", l, d, t))
                            if n:
                                pe.wait_ge(*at("ml_dst_read", l, d, n - 1, 1))
                                for hp in range(2):
                                    b = claim("ml_int", l, d, t, hp)
                                    for h in (2 * hp, 2 * hp + 1):
                                        i = mm(b[:, (h % 2) * 129:(h % 2) * 129 + 129], mqT[:, h, tc],
                                               cst[:, (n - 1) % 2, h, :])
                                    i.then_inc(*inc("ml_int", l, d, t, hp))
                            b = claim("ml_wT", l, d, t)
                            pe.wait_ge(*at("ml_qk_read", l, d, t))
                            for h in range(MH):
                                i = pe.transpose(b[:, h * P:(h + 1) * P], rW[:, h * P:(h + 1) * P], ident)
                            i.then_inc(*inc("ml_wT", l, d, t))
                            pe.wait_ge(*at("ml_wT_read", l, d, t))
                            for hp in range(2):
                                b = claim("ml_num", l, d, t, hp)
                                for h in (2 * hp, 2 * hp + 1):
                                    i = mm(b[:, (h % 2) * 129:(h % 2) * 129 + 129], rWT[:, h * P:(h + 1) * P],
                                           mv[:, t, h, :])
                                i.then_inc(*inc("ml_num", l, d, t, hp))
                        if n < NT - 1:
                            pe.wait_ge(*at("ml_kw", l, d, n))
                            for hp in range(2):
                                b = claim("ml_dst", l, d, n, hp)
                                for h in (2 * hp, 2 * hp + 1):
                                    i = mm(b[:, (h % 2) * 129:(h % 2) * 129 + 129], kw[:, h * P:(h + 1) * P],
                                           mv[:, t, h, :])
                                i.then_inc(*inc("ml_dst", l, d, n, hp))
                for t in outs(l):
                    b = claim("ml_T", l, t)
                    pe.wait_ge(*at("ml_norm", l, t))
                    for j in range(4):
                        i = pe.transpose(b[:, j * P:(j + 1) * P], acc[:, t, j * P:(j + 1) * P], ident)
                    i.then_inc(*inc("ml_T", l, t))
                if upto < 4:
                    break

                n = start["gate", l]
                for t in outs(l):
                    pe.wait_ge(*at("att_oT_read", l, t))
                    pe.wait_ge(*at("ssd_T_read", l, t))
                    pe.wait_ge(*at("ml_T_read", l, t))
                for pr in range(4):
                    for q in range(3):
                        w = split_slot(n, KB)
                        for j in range(2):
                            b = claim("gate", l, pr, 2 * q + j)
                            for k in range(KB):
                                pe.wait_ge(*at("x_low", "gate", l, k))
                                i = mm3(b[:, oc:T], [a[:, k, j * P:(j + 1) * P] for a in w],
                                        [x_high[:, k, oc:T], h_low[:, k, oc:T]], k == 0, k == KB - 1)
                            i.then_inc(*inc("gate", l, pr, 2 * q + j))
                        n += 1
                    for q in range(2):
                        w = split_slot(n, 12)
                        for r in range(3):
                            b = claim("proj", l, 2 * pr + q, r)
                            pe.wait_ge(*at("x_low", "branch", l, r))
                            for k in range(4):
                                i = mm3(b[:, oc:T], [a[:, 4 * r + k, :] for a in w],
                                        [br_high[:, r, k * T + oc:k * T + T], br_low[r][:, k, oc:T]],
                                        k == 0, k == 3)
                            i.then_inc(*inc("proj", l, 2 * pr + q, r))
                        n += 1
                for q in range(OUT_SLOTS):
                    w = split_slot(start["out", l] + q, KB)
                    for j in range(2):
                        b = claim("mix", l, 2 * q + j)
                        for k in range(KB):
                            pe.wait_ge(*at("x_low", "mix", l, k))
                            i = mm3(b[:, oc:T], [a[:, k, j * P:(j + 1) * P] for a in w],
                                    [x_high[:, k, oc:T], merged_low[:, k, oc:T]], k == 0, k == KB - 1)
                        i.then_inc(*inc("mix", l, 2 * q + j))
                if upto < 5:
                    break

                for pp in passes(l):
                    b = claim("ss2", pp)
                    for k in range(KB):
                        pe.wait_ge(*at("sq2", pp, k))
                        i = mm(b[:, 0:SEQ], ones, h2T[:, k, :], k == 0, k == KB - 1)
                    i.then_inc(*inc("ss2", pp))
                    for k in range(KB):
                        pe.wait_ge(*at("h2T", pp, k))
                    for q in range(WQ_SLOTS):
                        w = split_slot(start["wq", pp] + q, KB)
                        for j in range(2):
                            b = claim("pq", pp, 2 * q + j)
                            for k in range(KB):
                                pe.wait_ge(*at("x_low", "pq", pp, k))
                                i = mm3(b[:, 0:SEQ], [a[:, k, j * P:(j + 1) * P] for a in w],
                                        [h2q_high[:, k, :], h2q_low[:, k, :]], k == 0, k == KB - 1)
                            i.then_inc(*inc("pq", pp, 2 * q + j))
                    w = slot(start["sub", pp]).rearrange("p (k m) -> p k m", k=16)
                    pe.wait_ge(*at("pq_read", pp, 15))
                    for t in range(2):
                        for q in range(4):
                            b = claim("psc", pp, t, q)
                            for j in range(4):
                                hp = 4 * q + j
                                i = mm(b[:, j * P:(j + 1) * P], qpT[:, hp, t * P:(t + 1) * P], w[:, hp, :])
                            i.then_inc(*inc("psc", pp, t, q))
                    if pp == MOD_AHEAD:
                        mod_open(l + 1)
                    for t in range(2):
                        if pp == MOD_AHEAD:
                            mod_rows(l + 1, t * MOD_SLOTS // 2, (t + 1) * MOD_SLOTS // 2)
                        b = claim("route", pp, t)
                        pe.wait_ge(*at("sel", pp, t))
                        for j in range(3):
                            i = pe.transpose(b[:, j * P:(j + 1) * P], sel[:, j, :], ident)
                        i.then_inc(*inc("route", pp, t))
                    pinned.clear()
                    for b in range(8):
                        pe.wait_ge(*at(*holder[b]))
                        holder[b] = None
                    turn[0] = 0
                    if upto < 6:
                        break

                    g0 = passes_before(pp) * (SEQ // 4)
                    if g0 == 0:
                        pe.sem_inc(cnt.sem("g_product"), 2)
                        pe.sem_inc(cnt.sem("half_free"), 4)
                    with pe.Fori(0, SEQ // 8) as it:
                        for bf in range(2):
                            pe.wait_ge(cnt.sem("hot_ready"), it * 2 + (g0 + bf + 1))
                            pe.wait_ge(cnt.sem("g_bank_free"), it * 2 + (g0 + bf + 1))
                            for tt in range(4):
                                i = mm(ps[bf][:, tt * P:(tt + 1) * P], hot[:, bf, 0, tt, :], hot[:, bf, 1, tt, :])
                            i.then_inc(cnt.sem("g_product"), 1)
                    pe.wait_ge(cnt.sem("g_bank_free"), g0 + 2 + SEQ // 4)

                    pe.wait_ge(*at("zeros", pp))
                    pe.wait_ge(*at("h2lo", pp))
                    zeros = wt[:, 0, :, :].rearrange("p a b -> p (a b)")
                    for b in range(4):
                        i = mm(ps[b][:, :], h2hi[:, 0, 0:P], zeros)
                    i.then_inc(*inc("acc_clear", pp))
                    p = passes_before(pp)

                    def expert_in(it, c, par):
                        i_ = u_item(c)
                        pe.wait_ge(cnt.sem("u_bank_free"), it * 2 + (p * CHUNKS + c + 1))
                        for hf in range(2):
                            pe.wait_ge(cnt.sem("low_made"), it * 8 + (p * 2 * N_ITEMS + 2 * i_ + hf + 1))
                            w = halves[:, 2 * (i_ % 2) + hf, :, :].rearrange("p a (k m) -> p a k m", k=4)
                            for k in range(4):
                                kk = 4 * hf + k
                                o = ps[4 + par][:, 0:SEQ]
                                mm(o, w[:, 0, k, :], h2hi[:, kk, :], kk == 0, False)
                                mm(o, w[:, 0, k, :], h2lo[:, kk, :], False, False)
                                i = mm(o, w[:, 1, k, :], h2hi[:, kk, :], False, kk == KB - 1)
                            i.then_inc(cnt.sem("half_free"), 1)

                    def expert_out(it, c, par):
                        i_ = v_item(c)
                        pe.wait_ge(cnt.sem("w_ready"), it * 2 + (p * CHUNKS + c + 1))
                        for hf in range(2):
                            pe.wait_ge(cnt.sem("low_made"), it * 8 + (p * 2 * N_ITEMS + 2 * i_ + hf + 1))
                            w = halves[:, 2 * (i_ % 2) + hf, :, :].rearrange("p a (k m) -> p a k m", k=4)
                            for k in range(4):
                                j = 4 * hf + k
                                o = ps[j // 2][:, (j % 2) * SEQ:(j % 2) * SEQ + SEQ]
                                for a, b in ((0, 0), (0, 1), (1, 0)):
                                    i = pe.matmul(o, w[:, a, k, :], wt[:, par, b, :], start=False, stop=False,
                                                  skip_group_check=True)
                            i.then_inc(cnt.sem("half_free"), 1)

                    expert_in(0, 0, 0)
                    with pe.Fori(0, ITER) as it:
                        for c in range(2):
                            expert_in(it, c + 1, (c + 1) % 2)
                            expert_out(it, c, c)
                    c = CHUNKS - 2
                    expert_in(0, c + 1, 1)
                    expert_out(0, c, 0)
                    expert_out(0, c + 1, 1)
                    pe.wait_ge(*at("x_moe", pp))

        @block.scalar
        def _(act):
            def fn(o, i_, f, **kw_):
                return act.activation(o, i_, f, **kw_)

            def bank(topic, *key):
                act.wait_ge(*at(topic, *key))
                return ps[cnt.bank(topic, *key)]

            def split_high(n):
                act.wait_ge(cnt.sem(f"slot{n % SLOTS}"), 16 * (n // SLOTS + 1))
                j = split_items.index(n)
                if j >= 3:
                    topic, *key = items[split_items[j - 3]][2]
                    act.wait_ge(*at(topic, *key))
                fn(high_of(n), ring[:, n % SLOTS, 0:items[n][1]], ACT.Copy).then_inc(*inc("item_high", n))

            act.dma_start(wsm[:, 0, :, :], wsm_in[0]).then_inc(cnt.sem("wsm_in"), 16)
            act.dma_start(wsm[:, 1, :, :], wsm_in[1]).then_inc(cnt.sem("wsm_in"), 16)
            act.wait_ge(*at("c_in"))
            fn(csil[:, :, :], csil[:, :, :], ACT.Silu).then_inc(*inc("csil"))

            def mod_rows(l, first, end):
                for n in range(first, end):
                    b = bank("mod_row", l, n)
                    if n >= 2:
                        act.wait_ge(*at("mod_turn", l, n - 2))
                    fn(modrow[0:2, n % 2, :], b[0:2, 0:256], ACT.Copy).then_inc(*inc("mod_row_read", l, n))

            act.wait_ge(*at("x_in"))
            act.wait_ge(*at("vec_in"))
            for l in layers:
                if upto < 0:
                    break
                oc = cols(l)
                if l:
                    act.wait_ge(*at("x_moe", passes(l - 1)[-1]))
                for k in range(KB):
                    fn(hT[:, k, :], XT[:, k, :], ACT.Square).then_inc(*inc("sq1", l, k))
                if l == 0:
                    mod_rows(0, 0, MOD_SLOTS)
                act.wait_ge(*at("ss1_read", l))
                fn(rstd, rstd, ACT.Sqrt).then_inc(*inc("std1", l))
                for k in range(KB):
                    act.wait_ge(*at("xn1", l, k))
                    for s_ in range(2):
                        i = fn(hT[:, k, s_ * SEQ:(s_ + 1) * SEQ], hT[:, k, s_ * SEQ:(s_ + 1) * SEQ], ACT.Identity,
                               scale=scale1[:, k, s_:s_ + 1], bias=mod[:, l, k, s_:s_ + 1])
                    i.then_inc(*inc("hT", l, k))

                def qk(key, c0):
                    b = bank("fm", l, key)
                    if key != "k":
                        prev = "k" if key == ("q", 0) else ("q", key[1] - 1)
                        act.wait_ge(*at("qk_done", l, prev))
                    fn(qk_sq[:, c0:T], b[:, c0:T], ACT.Square).then_inc(*inc("qk_sq", l, key))
                    fn(qk_raw[:, c0:T], b[:, c0:T], ACT.Copy).then_inc(*inc("fm_read", l, key))
                    act.wait_ge(*at("qk_ss_read", l, key))
                    fn(qk_rs[:, c0:T], qk_rs[:, c0:T], ACT.Sqrt).then_inc(*inc("qk_std", l, key))

                b = bank("small", l)
                fn(sm.rearrange("p a b -> p (a b)"), b[:, 0:128], ACT.Copy).then_inc(*inc("small_read", l))
                qk_sq_first = "k"
                qk(qk_sq_first, 0)
                b = bank("v", l)
                fn(v_tm.rearrange("p a b -> p (a b)"), b[:, :], ACT.Copy).then_inc(*inc("v_read", l))
                for j in (4, 5, 0, 1, 2, 3):
                    b = bank("conv_in", l, j)
                    act.wait_ge(*at("pads", l))
                    fn(xin[:, j, :, 2:2 + SEQ], b[:, :].rearrange("p (a b) -> p a b", a=2), ACT.Copy
                       ).then_inc(*inc("conv_in_read", l, j))
                for n in range(4):
                    qk(("q", n), oc)
                for n in range(4):
                    b = bank("fm", l, ("mk", n))
                    fn(mkT[:, n, :], b[:, :], ACT.Copy, scale=MD ** -0.5).then_inc(*inc("fm_read", l, ("mk", n)))
                for n in range(4):
                    b = bank("fm", l, ("mq", n))
                    fn(mqT[:, n, oc:T], b[:, oc:T], ACT.Copy).then_inc(*inc("fm_read", l, ("mq", n)))
                for n in range(2):
                    for t in outs(l)[::2]:
                        b = bank("z", l, n, t)
                        fn(z[:, t:t + 2, n * 256:(n + 1) * 256], b[:, :].rearrange("p (a b) -> p a b", a=2), ACT.Silu
                           ).then_inc(*inc("z_read", l, n, t))
                for n in range(2):
                    for t in range(0, NT, 2):
                        b = bank("mv", l, n, t)
                        for tt in range(2):
                            i = fn(mv[:, t + tt, 2 * n:2 * n + 2, 0:MD],
                                   b[:, tt * 256:(tt + 1) * 256].rearrange("p (h e) -> p h e", h=2), ACT.Copy)
                        i.then_inc(*inc("mv_read", l, n, t))
                for n in range(2):
                    for t in outs(l)[::2]:
                        b = bank("mo", l, n, t)
                        fn(mo[:, t:t + 2, n * 256:(n + 1) * 256], b[:, :].rearrange("p (a b) -> p a b", a=2),
                           ACT.Sigmoid).then_inc(*inc("mo_read", l, n, t))
                for j in (4, 5, 0, 1, 2, 3):
                    act.wait_ge(*at("conv_acc", l, j))
                    fn(xcv[:, j, :], xcv[:, j, :], ACT.Silu, bias=vec[:, l, V_CB + j:V_CB + j + 1]
                       ).then_inc(*inc("conv", l, j))
                for t in range(NT):
                    b = bank("mk_t", l, t)
                    fn(mk_tm[:, t, :], b[:, :], ACT.Copy).then_inc(*inc("mk_t_read", l, t))
                for t in range(NT):
                    b = bank("xs_t", l, t)
                    fn(xs_tm[:, t, :], b[:, :], ACT.Copy).then_inc(*inc("xs_t_read", l, t))
                b = bank("B_t", l)
                fn(B_tm.rearrange("p a b -> p (a b)"), b[:, :], ACT.Copy).then_inc(*inc("B_t_read", l))
                act.wait_ge(*at("absx", l))
                fn(lnp[:, :, :], ab[:, :, :], ACT.Exp, scale=-1.0).then_inc(*inc("ssd_exp", "expx", l))
                fn(negA, vec[:, l, V_ALOG:V_ALOG + 16], ACT.Exp).then_inc(*inc("ssd_exp", "expA", l))
                act.wait_ge(*at("onep", l))
                fn(lnp[:, :, :], lnp[:, :, :], ACT.Ln).then_inc(*inc("ssd_exp", "lnx", l))
                act.wait_ge(*at("decays", "cm", l))
                fn(ecm[:, :, :], cm[:, :, 0:16], ACT.Exp).then_inc(*inc("ssd_exp", "ecm", l))
                fn(etot[:, :, :], cums[:, 2, :, 0:16], ACT.Exp).then_inc(*inc("ssd_exp", "etot", l))
                fn(dw[:, :, :], dw[:, :, :], ACT.Exp).then_inc(*inc("ssd_exp", "edw", l))
                if upto < 1:
                    break

                for t in outs(l):
                    keys = T if t >= 2 else SEQ
                    for h in range(AH):
                        b = ps[cnt.bank("att_s", l, t, h)]
                        act.wait_ge(*at("att_max", l, t, h))
                        if h >= 2:
                            act.wait_ge(*at("att_t", l, t, h - 2))
                        elif t != outs(l)[0]:
                            act.wait_ge(*at("att_t", l, t - 1, AH - 2 + h))
                        fn(att_p[:, h % 2, 0:keys], b[:, 0:keys], ACT.Exp, scale=AD ** -0.5,
                           bias=mx[:, t, h:h + 1], accum_out=rsum[:, t, h:h + 1]).then_inc(*inc("att_s_read", l, t, h))
                    b = bank("att_oT", l, t)
                    fn(attT[:, :, t * P:(t + 1) * P], b[:, :].rearrange("p (a b) -> p a b", a=4), ACT.Copy
                       ).then_inc(*inc("att_oT_read", l, t))
                if upto < 2:
                    break

                for d in range(2):
                    for n, t in enumerate(ORDER[d]):
                        if t in outs(l):
                            for g in range(2):
                                act.wait_ge(*at("ssd_row_read", l, d, t, g))
                                fn(dmat, dmat, ACT.Exp).then_inc(*inc("ssd_L", l, d, t, g))
                for t in outs(l):
                    act.wait_ge(*at("ssd_yz", l, t))
                    fn(yo, acc[:, t, :], ACT.Square, accum_out=rsum[:, t, 0:1]).then_inc(*inc("ssd_sq", l, t))
                    act.wait_ge(*at("ssd_var", l, t))
                    fn(rinv[:, t, 0:1], rinv[:, t, 0:1], ACT.Sqrt).then_inc(*inc("ssd_std", l, t))
                for t in outs(l):
                    b = bank("ssd_T", l, t)
                    for j in range(4):
                        i = fn(ssdT[:, j, t * P:(t + 1) * P], b[:, j * P:(j + 1) * P], ACT.Copy,
                               scale=vec[:, l, V_SSDN + j:V_SSDN + j + 1])
                    i.then_inc(*inc("ssd_T_read", l, t))
                if upto < 3:
                    break

                for d in range(2):
                    for n, t in enumerate(ORDER[d]):
                        if t in outs(l):
                            act.wait_ge(*at("ml_d", l, d, t))
                            fn(rW, rD, ACT.Exp).then_inc(*inc("ml_w", l, d, t))
                            fn(sml[:, 0, 4:6, :], sml[:, 0, 4:6, :], ACT.Exp).then_inc(*inc("ml_we", l, d, t))
                            b = bank("ml_wT", l, d, t)
                            fn(rWT, b[:, :], ACT.Copy).then_inc(*inc("ml_wT_read", l, d, t))
                            if n:
                                for hp in range(2):
                                    b = bank("ml_int", l, d, t, hp)
                                    fn(inter[:, 2 * hp:2 * hp + 2, :],
                                       b[:, 0:258].rearrange("p (a b) -> p a b", a=2), ACT.Copy
                                       ).then_inc(*inc("ml_int_read", l, d, t, hp))
                        if n < NT - 1:
                            act.wait_ge(*at("ml_g", l, d, n))
                            fn(sml[:, 1, 4:6, :], sml[:, 1, 4:6, :], ACT.Exp).then_inc(*inc("ml_eg", l, d, n))
                for t in outs(l):
                    act.wait_ge(*at("ml_var", l, t))
                    fn(rinv[:, t, 0:4], rinv[:, t, 0:4], ACT.Sqrt).then_inc(*inc("ml_std", l, t))
                for t in outs(l):
                    b = bank("ml_T", l, t)
                    for j in range(4):
                        i = fn(mlT[:, j, t * P:(t + 1) * P], b[:, j * P:(j + 1) * P], ACT.Copy,
                               scale=vec[:, l, V_MLN + j:V_MLN + j + 1])
                    i.then_inc(*inc("ml_T_read", l, t))
                if upto < 4:
                    break

                act.wait_ge(*at("ml_T", l, outs(l)[-1]))
                for k in range(KB):
                    fn(x_high[:, k, oc:T], hT[:, k, oc:T], ACT.Copy).then_inc(*inc("x_high", "gate", l, k))
                    if k < 3:
                        split_high(merge_item(l, k))
                act.wait_ge(*at("ml_T_read", l, outs(l)[-1]))
                for r, br in enumerate((attT, ssdT, mlT)):
                    fn(br_high[:, r, :].rearrange("p (a b) -> p a b", a=4)[:, :, oc:T], br[:, :, oc:T], ACT.Copy
                       ).then_inc(*inc("x_high", "branch", l, r))
                for pr in range(4):
                    for q in range(6):
                        b = bank("gate", l, pr, q)
                        if pr:
                            act.wait_ge(*at("proj_add", l, 2 * pr - 1, 2))
                        fn(gsig[:, q, oc:T], b[:, oc:T], ACT.Sigmoid).then_inc(*inc("gate_read", l, pr, q))
                        if q % 2:
                            split_high(merge_item(l, 5 * pr + q // 2 + 3))
                    for q in range(2):
                        split_high(merge_item(l, 5 * pr + 3 + q + 3))
                for k in range(KB):
                    act.wait_ge(*at("proj_add", l, k, 2))
                    fn(x_high[:, k, oc:T], mergedT[:, k, oc:T], ACT.Copy).then_inc(*inc("x_high", "mix", l, k))
                split_high(merge_item(l, 23))
                if upto < 5:
                    break

                for pp in passes(l):
                    s_ = pp[1]
                    tok = slice(s_ * SEQ, (s_ + 1) * SEQ)
                    act.wait_ge(*at("mix_read", l, KB - 1))
                    if s_ and l < DEPTH - 1:
                        act.wait_ge(*at("x_moe", (l, 0)))
                    for k in range(KB):
                        fn(h2T[:, k, :], XT[:, k, tok], ACT.Square).then_inc(*inc("sq2", pp, k))
                    for n in range(3):
                        split_high(start["wq", pp] + n)
                    act.wait_ge(*at("ss2_read", pp))
                    fn(rstd2, rstd2, ACT.Sqrt).then_inc(*inc("std2", pp))
                    for k in range(KB):
                        act.wait_ge(*at("xn2", pp, k))
                        fn(h2T[:, k, :], h2T[:, k, :], ACT.Identity, scale=scale2[:, k, s_:s_ + 1],
                           bias=mod[:, l, 24 + k, s_:s_ + 1]).then_inc(*inc("h2T", pp, k))
                        act.wait_ge(*at("h2T", pp, k))
                        fn(h2q_high[:, k, :], h2T[:, k, :], ACT.Copy).then_inc(*inc("x_high", "pq", pp, k))
                    for j in range(16):
                        b = bank("pq", pp, j)
                        fn(qpT[:, j, :], b[:, 0:SEQ], ACT.Copy).then_inc(*inc("pq_read", pp, j))
                        if j % 2 and j // 2 + 3 < WQ_SLOTS:
                            split_high(start["wq", pp] + j // 2 + 3)
                    for t in range(2):
                        for q in range(4):
                            b = bank("psc", pp, t, q)
                            fn(scs[t][:, 4 * q:4 * q + 4, :], b[:, :].rearrange("p (a b) -> p a b", a=4), ACT.Copy
                               ).then_inc(*inc("psc_read", pp, t, q))
                    for t in range(2):
                        if pp == MOD_AHEAD:
                            mod_rows(l + 1, t * MOD_SLOTS // 2, (t + 1) * MOD_SLOTS // 2)
                        act.wait_ge(*at("gate_e", pp, t))
                        fn(sc16[:, :, :], sc16[:, :, :], ACT.Exp).then_inc(*inc("gate_x", pp, t))
                        b = bank("route", pp, t)
                        fn(RT[:, :, t * P:(t + 1) * P], b[:, 0:384].rearrange("p (a b) -> p a b", a=3), ACT.Copy
                           ).then_inc(*inc("route_read", pp, t))
                    if upto < 6:
                        break
                    g0 = passes_before(pp) * (SEQ // 4)
                    if g0 == 0:
                        act.sem_inc(cnt.sem("g_bank_free"), 2)
                    with act.Fori(0, SEQ // 8) as it:
                        for bf in range(2):
                            act.wait_ge(cnt.sem("g_product"), it * 2 + (g0 + bf + 3))
                            act.activation(
                                G[:, :, bass.ds(it * 8 + 4 * bf, 4)].rearrange("p i t -> p t i"),
                                ps[bf][:, :].rearrange("p (t i) -> p t i", t=4), ACT.Copy,
                            ).then_inc(cnt.sem("g_bank_free"), 1)
                    p = passes_before(pp)
                    act.wait_ge(cnt.sem("g_product"), g0 + 2 + SEQ // 4)
                    fn(h2hi[:, :, :], h2T[:, :, :], ACT.Copy).then_inc(*inc("h2hi", pp))
                    if p == 0:
                        act.sem_inc(cnt.sem("u_bank_free"), 2)

                    def high(it, i_):
                        act.wait_ge(cnt.sem(f"raw{i_ % 4}"), it * 16 + 16 * (64 * p + i_ // 4 + 1))
                        for hf in range(2):
                            act.wait_ge(cnt.sem("half_free"), it * 8 + (p * 2 * N_ITEMS + 2 * i_ + hf + 1))
                            act.activation(halves[:, 2 * (i_ % 2) + hf, 0, :], raw[:, i_ % 4, hf * HALF:(hf + 1) * HALF],
                                           ACT.Copy).then_inc(cnt.sem("high_made"), 1)

                    def gelu(it, c, par):
                        act.wait_ge(cnt.sem("half_free"), it * 8 + (p * 2 * N_ITEMS + 2 * u_item(c) + 6))
                        act.wait_ge(cnt.sem("ge_free"), it * 2 + (p * CHUNKS + c + 1))
                        act.activation(ge, ps[4 + par][:, 0:SEQ], ACT.Gelu_apprx_tanh
                                       ).then_inc(cnt.sem("u_bank_free"), 1)

                    high(0, 0)
                    high(0, 1)
                    gelu(0, 0, 0)
                    high(0, 2)
                    with act.Fori(0, ITER) as it:
                        for c in (1, 2):
                            high(it, u_item(c + 1))
                            gelu(it, c, c % 2)
                            high(it, v_item(c))
                    gelu(0, CHUNKS - 1, 1)
                    high(0, N_ITEMS - 1)

        @block.vector
        def _(dve):
            steps = [0]

            def link(ins):
                steps[0] += 1
                ins.then_inc(cnt.sem("dve_step"), 1)
                dve.wait_ge(cnt.sem("dve_step"), steps[0])

            def bank(topic, *key):
                dve.wait_ge(*at(topic, *key))
                return ps[cnt.bank(topic, *key)]

            def tt(o, a, b, op):
                return dve.tensor_tensor(o, a, b, op)

            def over(a, n):
                return a.unsqueeze(len(a.shape)).broadcast_to([*a.shape, n])

            def rep(a, n):
                return a.unsqueeze(1).broadcast_to([a.shape[0], n, *a.shape[1:]])

            def split_low(n):
                dve.wait_ge(*at("item_high", n))
                tt(low_of(n), ring[:, n % SLOTS, 0:items[n][1]], high_of(n).bitcast(F32), ALU.subtract
                   ).then_inc(*inc("item_low", n))

            def modulation(l):
                dve.wait_ge(*at("mod_turn", l, MOD_SLOTS - 1))
                b = ps[cnt.bank("mod", l)]
                tt(mod[:, l, :, :], b[:, 0:96].rearrange("p (a b) -> p a b", b=2),
                   over(vec[:, l, V_BMOD:V_BMOD + 48], 2), ALU.add).then_inc(*inc("mod_read", l))
                dve.wait_ge(*at("mod_read", l))

            dve.wait_ge(*at("vec_in"))
            dve.wait_ge(*at("const_in"))
            for l in layers:
                if upto < 0:
                    break
                oc = cols(l)
                if l == 0:
                    modulation(0)
                for m, s_, v in ((8, scale1, V_N1), (32, scale2, V_N2)):
                    link(dve.tensor_scalar(s_[:, :, :], mod[:, l, m:m + 8, :], 1.0, None, ALU.add))
                    link(tt(s_[:, :, :], s_[:, :, :], over(vec[:, l, v:v + 8], 2), ALU.mult))
                link(dve.memset(xin[:, :, :, 0:2], 0.0))
                dve.memset(xin[:, :, :, 2 + SEQ:XPAD], 0.0).then_inc(*inc("pads", l))
                link(dve.memset(mv[:, :, :, MD:MD + 1], 1.0))
                b = bank("ss1", l)
                dve.tensor_scalar(rstd, b[:, :], 1.0 / D, EPS, ALU.mult, ALU.add).then_inc(*inc("ss1_read", l))
                dve.wait_ge(*at("ss1_read", l))
                dve.wait_ge(*at("std1", l))
                link(dve.reciprocal(rstd, rstd))
                for k in range(KB):
                    tt(hT[:, k, :], XT[:, k, :], rstd, ALU.mult).then_inc(*inc("xn1", l, k))

                b = None
                dve.wait_ge(*at("small_read", l))
                link(tt(sm[:, :, :], sm[:, :, :], rep(vec[:, l, V_BIAS:V_BIAS + 32], NT), ALU.add))
                dve.scalar_tensor_tensor(out=ab[:, :, :], in0=sm[:, :, :], scalar=-1.0, in1=sm[:, :, :],
                                         op0=ALU.mult, op1=ALU.max).then_inc(*inc("absx", l))

                def qk(key, c0, o, norm_col):
                    w = T - c0
                    b = bank("qk_ss", l, key)
                    dve.tensor_scalar(qk_rs[:, c0:T], b[:, c0:T], 1.0 / AD, EPS, ALU.mult, ALU.add
                                      ).then_inc(*inc("qk_ss_read", l, key))
                    dve.wait_ge(*at("qk_ss_read", l, key))
                    dve.wait_ge(*at("qk_std", l, key))
                    link(dve.reciprocal(qk_rs[:, c0:T], qk_rs[:, c0:T]))
                    dve.wait_ge(*at("fm_read", l, key))
                    dve.scalar_tensor_tensor(out=qk_n[:, c0:T], in0=qk_raw[:, c0:T],
                                             scalar=vec[:, l, norm_col:norm_col + 1], in1=qk_rs[:, c0:T],
                                             op0=ALU.mult, op1=ALU.mult).then_inc(*inc("qk_n", l, key))
                    dve.wait_ge(*at("qk_n", l, key))
                    if c0 == 0:
                        dve.tensor_copy(o[:, 0:SEQ], qk_n[:, 0:SEQ])
                    link(tt(qk_t[:, SEQ:T], qk_n[:, SEQ:T], const[:, C_COS:C_COS + SEQ], ALU.mult))
                    b = bank("qk_swap", l, key)
                    tt(qk_t[:, 0:SEQ], b[:, 0:SEQ], const[:, C_SIN:C_SIN + SEQ], ALU.mult
                       ).then_inc(*inc("qk_swap_read", l, key))
                    dve.wait_ge(*at("qk_swap_read", l, key))
                    tt(o[:, SEQ:T], qk_t[:, SEQ:T], qk_t[:, 0:SEQ], ALU.add).then_inc(*inc("qk_done", l, key))

                qk("k", 0, kT, V_KN)
                for n in range(4):
                    qk(("q", n), oc, qT[:, n, :], V_QN)

                for j in (4, 5, 0, 1, 2, 3):
                    dve.wait_ge(*at("conv_in_read", l, j))
                    o = xcv[:, j, :].rearrange("p (a b) -> p a b", a=2)
                    for tap in range(TAPS):
                        w = vec[:, l, V_CW + j * TAPS + tap:V_CW + j * TAPS + tap + 1]
                        x_ = xin[:, j, :, tap:tap + SEQ]
                        if tap == 0:
                            i = dve.tensor_scalar(o, x_, w, None, ALU.mult)
                        else:
                            i = dve.scalar_tensor_tensor(out=o, in0=x_, scalar=w, in1=o, op0=ALU.mult, op1=ALU.add)
                        if tap < TAPS - 1:
                            link(i)
                    i.then_inc(*inc("conv_acc", l, j))

                dve.wait_ge(*at("ssd_exp", "expx", l))
                dve.tensor_scalar(lnp[:, :, :], lnp[:, :, :], 1.0, None, ALU.add).then_inc(*inc("onep", l))
                dve.wait_ge(*at("ssd_exp", "expA", l))
                link(dve.tensor_scalar(negA, negA, -1.0, None, ALU.mult))
                dve.wait_ge(*at("ssd_exp", "lnx", l))
                link(dve.tensor_scalar(dt[:, :, :], sm[:, :, 0:16], 0.0, None, ALU.max))
                link(tt(dt[:, :, :], dt[:, :, :], lnp[:, :, 0:16], ALU.add))
                link(tt(dec[:, :, 0:16], dt[:, :, :], rep(negA, NT), ALU.mult))
                for d in range(2):
                    f = slice(16 + d * 8 + 4, 16 + d * 8 + 8)
                    i = dve.scalar_tensor_tensor(out=dec[:, :, 16 + 4 * d:20 + 4 * d], in0=sm[:, :, f], scalar=0.0,
                                                 in1=lnp[:, :, f], op0=ALU.min, op1=ALU.subtract)
                    link(i)
                dve.sem_inc(*inc("decays", "dec", l))
                b = bank("cums", l)
                dve.tensor_copy(cums[:, :, :, :], b[:, 0:3 * NT * NG].rearrange("p (a b c) -> p a b c", a=3, b=NT)
                                ).then_inc(*inc("cums_read", l))
                dve.wait_ge(*at("cums_read", l))
                for n, (a, e) in ((0, (0, 8)), (1, (8, 16)), (0, (16, 20)), (1, (20, 24))):
                    link(dve.tensor_copy(cm[:, :, a:e], cums[:, n, :, a:e]))
                link(tt(dw[:, :, :], cums[:, 2, :, 0:16], cm[:, :, 0:16], ALU.subtract))
                for d in range(2):
                    link(tt(rr[:, :, 4 * d:4 * d + 4], sm[:, :, 16 + 8 * d:20 + 8 * d], cm[:, :, 16 + 4 * d:20 + 4 * d],
                            ALU.subtract))
                dve.sem_inc(*inc("decays", "cm", l))
                dve.wait_ge(*at("ssd_exp", "edw", l))
                link(tt(dw[:, :, :], dw[:, :, :], dt[:, :, :], ALU.mult))
                if upto < 1:
                    break

                for t in outs(l):
                    keys = T if t >= 2 else SEQ

                    def smax(h):
                        b = bank("att_s", l, t, h)
                        link(dve.tensor_reduce(mx[:, t, h:h + 1], b[:, 0:keys], AX.X, ALU.max, negate=True))
                        dve.tensor_scalar(mx[:, t, h:h + 1], mx[:, t, h:h + 1], AD ** -0.5, None, ALU.mult
                                          ).then_inc(*inc("att_max", l, t, h))

                    smax(0)
                    for h in range(AH):
                        if h + 1 < AH:
                            smax(h + 1)
                        b = bank("att_t", l, t, h)
                        if h >= 2:
                            dve.wait_ge(*at("att_pv", l, t, h - 2))
                        elif t != outs(l)[0]:
                            dve.wait_ge(*at("att_pv", l, t - 1, AH - 2 + h))
                        dve.tensor_copy(att_pT[:, h % 2, 0:keys // P, :],
                                        b[:, 0:keys].rearrange("p (a b) -> p a b", b=P)
                                        ).then_inc(*inc("att_t_read", l, t, h))
                    dve.wait_ge(*at("att_s_read", l, t, AH - 1))
                    link(dve.reciprocal(rinv[:, t, :], rsum[:, t, :]))
                    dve.wait_ge(*at("att_pv", l, t, AH - 1))
                    b = ps[cnt.bank("att_o", l, t)]
                    tt(acc[:, t, :].rearrange("p (h e) -> p h e", h=AH), b[:, :].rearrange("p (h e) -> p h e", h=AH),
                       over(rinv[:, t, :], AD), ALU.mult).then_inc(*inc("att_o_read", l, t))
                if upto < 2:
                    break

                dve.wait_ge(*at("ssd_exp", "etot", l))
                for t in outs(l):
                    dve.wait_ge(*at("att_oT_read", l, t))
                dve.wait_ge(*at("xs_t_read", l, NT - 1))
                for d in range(2):
                    for n, t in enumerate(ORDER[d]):
                        xs3 = xs_tm[:, t, :].rearrange("p (h e) -> p h e", h=SH)
                        a3 = acc[:, t, :].rearrange("p (h e) -> p h e", h=SH)
                        dh = slice(d * 8, d * 8 + 8)
                        if t in outs(l):
                            for g in range(2):
                                b = bank("ssd_cb", l, d, t, g)
                                dve.tensor_copy(cb[:, g * P:(g + 1) * P], b[:, 0:P]
                                                ).then_inc(*inc("ssd_cb_read", l, d, t, g))
                                dve.wait_ge(*at("ssd_cb_read", l, d, t, g))
                            link(tt(xc.rearrange("p (h e) -> p h e", h=SH), xs3, over(dt[:, t, dh], SD), ALU.mult))
                            for g in range(2):
                                b = bank("ssd_row", l, d, t, g)
                                for j in range(4):
                                    h = d * 8 + g * 4 + j
                                    i = dve.scalar_tensor_tensor(out=dmat[:, j * P:(j + 1) * P],
                                                                 in0=b[:, j * P:(j + 1) * P],
                                                                 scalar=cm[:, t, h:h + 1], in1=nmask[d],
                                                                 op0=ALU.subtract, op1=ALU.add)
                                i.then_inc(*inc("ssd_row_read", l, d, t, g))
                                dve.wait_ge(*at("ssd_row_read", l, d, t, g))
                                dve.wait_ge(*at("ssd_L", l, d, t, g))
                                if g:
                                    dve.wait_ge(*at("ssd_mm", l, d, t, 0))
                                tt(mmat.rearrange("p (a b) -> p a b", a=4), dmat.rearrange("p (a b) -> p a b", a=4),
                                   rep(cb[:, g * P:(g + 1) * P], 4), ALU.mult).then_inc(*inc("ssd_m", l, d, t, g))
                                dve.wait_ge(*at("ssd_m", l, d, t, g))
                            first = d == 0
                            if first:
                                link(tt(a3, xs3, over(vec[:, l, V_D:V_D + 8], SD), ALU.mult))
                            if n:
                                for g in range(2):
                                    b = bank("ssd_off", l, d, t, g)
                                    tt(yo[:, g * 256:(g + 1) * 256].rearrange("p (h e) -> p h e", h=4),
                                       b[:, 0:256].rearrange("p (h e) -> p h e", h=4),
                                       over(ecm[:, t, d * 8 + 4 * g:d * 8 + 4 * g + 4], SD), ALU.mult
                                       ).then_inc(*inc("ssd_off_read", l, d, t, g))
                                    dve.wait_ge(*at("ssd_off_read", l, d, t, g))
                                dve.wait_ge(*at("ssd_off_read", l, d, t, 1))
                                link(tt(acc[:, t, :], acc[:, t, :], yo, ALU.add))
                            dve.wait_ge(*at("ssd_mm", l, d, t, 1))
                            b = ps[cnt.bank("ssd_y", l, d, t)]
                            tt(acc[:, t, :], acc[:, t, :], b[:, :], ALU.add).then_inc(*inc("ssd_y_read", l, d, t))
                            dve.wait_ge(*at("ssd_y_read", l, d, t))
                        if n < NT - 1:
                            if n:
                                dve.wait_ge(*at("ssd_dst", l, d, n - 1))
                            elif d:
                                dve.wait_ge(*at("ssd_dst", l, 0, NT - 2))
                            tt(xd.rearrange("p (h e) -> p h e", h=SH), xs3, over(dw[:, t, dh], SD), ALU.mult
                               ).then_inc(*inc("ssd_xd", l, d, n))
                            dve.wait_ge(*at("ssd_xd", l, d, n))
                            b = bank("ssd_dst", l, d, n)
                            for g in range(2):
                                gp = slice(g * SN, g * SN + SN)
                                if n:
                                    link(tt(st[gp, n % 2, :].rearrange("p (h e) -> p h e", h=4),
                                            st[gp, (n - 1) % 2, :].rearrange("p (h e) -> p h e", h=4),
                                            over(etot[gp, t, d * 8 + 4 * g:d * 8 + 4 * g + 4], SD), ALU.mult))
                                    i = tt(st[gp, n % 2, :], st[gp, n % 2, :], b[gp, g * 256:(g + 1) * 256], ALU.add)
                                else:
                                    i = dve.tensor_copy(st[gp, n % 2, :], b[gp, g * 256:(g + 1) * 256])
                                if g == 0:
                                    link(i)
                            i.then_inc(*inc("ssd_dst_read", l, d, n))
                            dve.wait_ge(*at("ssd_dst_read", l, d, n))
                for t in outs(l):
                    if t == outs(l)[0]:
                        dve.wait_ge(*at("ssd_y_read", l, 1, ORDER[1][-1]))
                        for n in range(2):
                            dve.wait_ge(*at("z_read", l, n, 2))
                    tt(acc[:, t, :], acc[:, t, :], z[:, t, :], ALU.mult).then_inc(*inc("ssd_yz", l, t))
                    dve.wait_ge(*at("ssd_yz", l, t))
                for t in outs(l):
                    dve.wait_ge(*at("ssd_sq", l, t))
                    dve.tensor_scalar(rinv[:, t, 0:1], rsum[:, t, 0:1], 1.0 / 512, EPS, ALU.mult, ALU.add
                                      ).then_inc(*inc("ssd_var", l, t))
                    dve.wait_ge(*at("ssd_var", l, t))
                    dve.wait_ge(*at("ssd_std", l, t))
                    link(dve.reciprocal(rinv[:, t, 0:1], rinv[:, t, 0:1]))
                    dve.tensor_scalar(acc[:, t, :], acc[:, t, :], rinv[:, t, 0:1], None, ALU.mult
                                      ).then_inc(*inc("ssd_norm", l, t))
                    dve.wait_ge(*at("ssd_norm", l, t))
                if upto < 3:
                    break

                for t in outs(l):
                    dve.wait_ge(*at("ssd_T_read", l, t))
                dve.wait_ge(*at("mk_t_read", l, NT - 1))
                for d in range(2):
                    fc = slice(16 + 4 * d, 20 + 4 * d)
                    m_now = sml[:, 1, 0, :]
                    link(dve.memset(m_now, 0.0))
                    for n, t in enumerate(ORDER[d]):
                        rc = slice(4 * d, 4 * d + 4)
                        b = bank("ml_row", l, d, t)
                        rows = b[:, :].rearrange("p (a b) -> p a b", a=4)
                        i = dve.tensor_reduce(sml[:, 1, 1, :], rows, AX.X, ALU.max)
                        link(i)
                        if t in outs(l):
                            link(tt(rD.rearrange("p (a b) -> p a b", a=4), rows, rep(nmask[1 - d], 4), ALU.add))
                            rmax, mm_, wi, en = (sml[:, 0, 0, :], sml[:, 0, 1, :], sml[:, 0, 4, :], sml[:, 0, 5, :])
                            link(dve.tensor_reduce(rmax, rD.rearrange("p (a b) -> p a b", a=4), AX.X, ALU.max))
                            link(tt(mm_, rmax, m_now, ALU.max))
                            link(tt(rD.rearrange("p (a b) -> p a b", a=4), rD.rearrange("p (a b) -> p a b", a=4),
                                    over(mm_, P), ALU.subtract))
                            link(tt(wi, m_now, mm_, ALU.subtract))
                            link(tt(en, cm[:, t, fc], mm_, ALU.add))
                            dve.tensor_scalar(en, en, -1.0, None, ALU.mult).then_inc(*inc("ml_d", l, d, t))
                            dve.wait_ge(*at("ml_d", l, d, t))
                        dve.sem_inc(*inc("ml_row_read", l, d, t))
                        if t in outs(l):
                            dve.wait_ge(*at("ml_w", l, d, t))
                            b = bank("ml_qk", l, d, t)
                            tt(rW, b[:, :], rW, ALU.mult).then_inc(*inc("ml_qk_read", l, d, t))
                            dve.wait_ge(*at("ml_qk_read", l, d, t))
                        if n < NT - 1:
                            mloc, m_new, tot = sml[:, 1, 1, :], sml[:, 1, 2, :], cums[:, 2, t, fc]
                            ap_, wk = sml[:, 1, 4, :], sml[:, 1, 5, :]
                            link(tt(m_new, mloc, m_now, ALU.max))
                            link(tt(m_new, m_new, tot, ALU.add))
                            link(tt(ap_, m_now, tot, ALU.add))
                            link(tt(ap_, ap_, m_new, ALU.subtract))
                            link(tt(wk, rr[:, t, rc], tot, ALU.add))
                            tt(wk, wk, m_new, ALU.subtract).then_inc(*inc("ml_g", l, d, n))
                            dve.wait_ge(*at("ml_g", l, d, n))
                            link(dve.tensor_copy(m_now, m_new))
                            dve.wait_ge(*at("ml_eg", l, d, n))
                            if n:
                                dve.wait_ge(*at("ml_dst", l, d, n - 1, 1))
                            elif d:
                                dve.wait_ge(*at("ml_dst", l, 0, NT - 2, 1))
                            tt(kw.rearrange("p (a b) -> p a b", a=4), mk_tm[:, t, :].rearrange("p (a b) -> p a b", a=4),
                               over(wk, P), ALU.mult).then_inc(*inc("ml_kw", l, d, n))
                            dve.wait_ge(*at("ml_kw", l, d, n))
                            for hp in range(2):
                                b = bank("ml_dst", l, d, n, hp)
                                for h in (2 * hp, 2 * hp + 1):
                                    p_ = b[:, (h % 2) * 129:(h % 2) * 129 + 129]
                                    if n:
                                        i = dve.scalar_tensor_tensor(out=cst[:, n % 2, h, :],
                                                                     in0=cst[:, (n - 1) % 2, h, :],
                                                                     scalar=ap_[:, h:h + 1], in1=p_,
                                                                     op0=ALU.mult, op1=ALU.add)
                                    else:
                                        i = dve.tensor_copy(cst[:, n % 2, h, :], p_)
                                i.then_inc(*inc("ml_dst_read", l, d, n, hp))
                                dve.wait_ge(*at("ml_dst_read", l, d, n, hp))
                            dve.wait_ge(*at("ml_dst_read", l, d, n, 1))
                        if t in outs(l):
                            dve.wait_ge(*at("ml_we", l, d, t))
                            for hp in range(2):
                                b = bank("ml_num", l, d, t, hp)
                                if n:
                                    dve.wait_ge(*at("ml_int_read", l, d, t, hp))
                                for h in (2 * hp, 2 * hp + 1):
                                    p_ = b[:, (h % 2) * 129:(h % 2) * 129 + 129]
                                    if n:
                                        i = dve.scalar_tensor_tensor(out=numt[:, h, :], in0=inter[:, h, :],
                                                                     scalar=wi[:, h:h + 1], in1=p_,
                                                                     op0=ALU.mult, op1=ALU.add)
                                    else:
                                        i = dve.tensor_copy(numt[:, h, :], p_)
                                i.then_inc(*inc("ml_num_read", l, d, t, hp))
                                dve.wait_ge(*at("ml_num_read", l, d, t, hp))
                            dve.wait_ge(*at("ml_num_read", l, d, t, 1))
                            den = sml[:, 0, 2, :]
                            d_ = numt[:, :, MD:MD + 1].rearrange("p a b -> p (a b)")
                            link(dve.scalar_tensor_tensor(out=den, in0=d_, scalar=-1.0, in1=d_, op0=ALU.mult,
                                                          op1=ALU.max))
                            link(tt(den, den, en, ALU.max))
                            link(dve.reciprocal(den, den))
                            a3 = acc[:, t, :].rearrange("p (a b) -> p a b", a=4)
                            if d == 0:
                                link(tt(a3, numt[:, :, 0:MD], over(den, MD), ALU.mult))
                            else:
                                link(tt(numt[:, :, 0:MD], numt[:, :, 0:MD], over(den, MD), ALU.mult))
                                link(tt(a3, a3, numt[:, :, 0:MD], ALU.add))
                for t in outs(l):
                    a3 = acc[:, t, :].rearrange("p (a b) -> p a b", a=4)
                    link(tt(rD, acc[:, t, :], acc[:, t, :], ALU.mult))
                    link(dve.tensor_reduce(rinv[:, t, 0:4], rD.rearrange("p (a b) -> p a b", a=4), AX.X, ALU.add))
                    dve.tensor_scalar(rinv[:, t, 0:4], rinv[:, t, 0:4], 1.0 / MD, EPS, ALU.mult, ALU.add
                                      ).then_inc(*inc("ml_var", l, t))
                    dve.wait_ge(*at("ml_var", l, t))
                for n in range(2):
                    dve.wait_ge(*at("mo_read", l, n, 2))
                for t in outs(l):
                    a3 = acc[:, t, :].rearrange("p (a b) -> p a b", a=4)
                    dve.wait_ge(*at("ml_std", l, t))
                    link(dve.reciprocal(rinv[:, t, 0:4], rinv[:, t, 0:4]))
                    link(tt(a3, a3, over(rinv[:, t, 0:4], MD), ALU.mult))
                    tt(acc[:, t, :], acc[:, t, :], mo[:, t, :], ALU.mult).then_inc(*inc("ml_norm", l, t))
                    dve.wait_ge(*at("ml_norm", l, t))
                if upto < 4:
                    break

                for k in range(KB):
                    dve.wait_ge(*at("x_high", "gate", l, k))
                    tt(h_low[:, k, oc:T], hT[:, k, oc:T], x_high[:, k, oc:T].bitcast(F32), ALU.subtract
                       ).then_inc(*inc("x_low", "gate", l, k))
                    if k < 3:
                        split_low(merge_item(l, k))
                for r, br in enumerate((attT, ssdT, mlT)):
                    dve.wait_ge(*at("x_high", "branch", l, r))
                    tt(br_low[r][:, :, oc:T], br[:, :, oc:T],
                       br_high[:, r, :].bitcast(F32).rearrange("p (a b) -> p a b", a=4)[:, :, oc:T], ALU.subtract
                       ).then_inc(*inc("x_low", "branch", l, r))
                for db in range(KB):
                    if db % 2 == 0:
                        for n in range(3):
                            split_low(merge_item(l, 5 * (db // 2) + 3 + n))
                    m = mergedT[:, db, oc:T]
                    for r in range(3):
                        q = (db % 2) * 3 + r
                        b = bank("proj", l, db, r)
                        dve.wait_ge(*at("gate_read", l, db // 2, q))
                        if r == 0:
                            i = tt(m, b[:, oc:T], gsig[:, q, oc:T], ALU.mult)
                        else:
                            i = tt(gsig[:, q, oc:T], b[:, oc:T], gsig[:, q, oc:T], ALU.mult)
                        i.then_inc(*inc("proj_read", l, db, r))
                        dve.wait_ge(*at("proj_read", l, db, r))
                        if r:
                            tt(m, m, gsig[:, q, oc:T], ALU.add).then_inc(*inc("proj_add", l, db, r))
                            dve.wait_ge(*at("proj_add", l, db, r))
                    split_low(merge_item(l, 5 * (db // 2) + 3 + db % 2 + 3))
                for k in range(KB):
                    dve.wait_ge(*at("x_high", "mix", l, k))
                    tt(merged_low[:, k, oc:T], mergedT[:, k, oc:T], x_high[:, k, oc:T].bitcast(F32),
                       ALU.subtract).then_inc(*inc("x_low", "mix", l, k))
                split_low(merge_item(l, 23))
                streams = [0, 1] if l < DEPTH - 1 else [1]
                for j in range(KB):
                    b = bank("mix", l, j)
                    for s_ in streams:
                        tok = slice(s_ * SEQ, (s_ + 1) * SEQ)
                        i = dve.scalar_tensor_tensor(out=XT[:, j, tok], in0=b[:, tok],
                                                     scalar=mod[:, l, 16 + j, s_:s_ + 1], in1=XT[:, j, tok],
                                                     op0=ALU.mult, op1=ALU.add)
                    i.then_inc(*inc("mix_read", l, j))
                dve.wait_ge(*at("mix_read", l, KB - 1))
                if upto < 5:
                    break

                for pp in passes(l):
                    s_ = pp[1]
                    tok = slice(s_ * SEQ, (s_ + 1) * SEQ)
                    b = bank("ss2", pp)
                    dve.tensor_scalar(rstd2, b[:, 0:SEQ], 1.0 / D, EPS, ALU.mult, ALU.add
                                      ).then_inc(*inc("ss2_read", pp))
                    dve.wait_ge(*at("ss2_read", pp))
                    dve.wait_ge(*at("std2", pp))
                    link(dve.reciprocal(rstd2, rstd2))
                    for k in range(KB):
                        tt(h2T[:, k, :], XT[:, k, tok], rstd2, ALU.mult).then_inc(*inc("xn2", pp, k))
                    for n in range(3):
                        split_low(start["wq", pp] + n)
                    for k in range(KB):
                        dve.wait_ge(*at("x_high", "pq", pp, k))
                        tt(h2q_low[:, k, :], h2T[:, k, :], h2q_high[:, k, :].bitcast(F32), ALU.subtract
                           ).then_inc(*inc("x_low", "pq", pp, k))
                    for n in range(3, WQ_SLOTS):
                        split_low(start["wq", pp] + n)
                    for t in range(2):
                        dve.wait_ge(*at("psc_read", pp, t, 3))
                        sc = scs[t]
                        i16u = i16.bitcast(U32)
                        for o in (0, 8):
                            for hp in range(16):
                                i = dve.max(v16[:, hp, o:o + 8], sc[:, hp, :])
                            link(i)
                            for hp in range(16):
                                i = dve.max_index(i16u[:, hp, o:o + 8], v16[:, hp, o:o + 8], sc[:, hp, :])
                            link(i)
                            if o == 0:
                                for hp in range(16):
                                    i = dve.match_replace(sc[:, hp, :], v16[:, hp, 0:8], sc[:, hp, :], -3e38)
                                link(i)
                        link(dve.tensor_copy(i16f[:, :, :], i16u))
                        v4 = v16[:, :, :].rearrange("p (h q) k -> p h q k", q=2)
                        link(tt(cand.rearrange("p h (a b) -> p h a b", a=TOPK),
                                v4[:, :, 0, :].unsqueeze(3).broadcast_to([P, PH, TOPK, TOPK]),
                                v4[:, :, 1, :].unsqueeze(2).broadcast_to([P, PH, TOPK, TOPK]), ALU.add))
                        posu = pos.bitcast(U32)
                        for o in (0, 8):
                            for h in range(PH):
                                i = dve.max(sc16[:, h, o:o + 8], cand[:, h, :])
                            link(i)
                            for h in range(PH):
                                i = dve.max_index(posu[:, h, o:o + 8], sc16[:, h, o:o + 8], cand[:, h, :])
                            link(i)
                            if o == 0:
                                for h in range(PH):
                                    i = dve.match_replace(cand[:, h, :], sc16[:, h, 0:8], cand[:, h, :], -3e38)
                                link(i)
                        link(dve.tensor_copy(g8, sc16[:, :, 0:1].rearrange("p a b -> p (a b)")))
                        tt(sc16[:, :, :], sc16[:, :, :], over(g8, TOPK), ALU.subtract).then_inc(*inc("gate_e", pp, t))
                        link(dve.tensor_scalar(pa.bitcast(U32), posu, 4, None, ALU.logical_shift_right))
                        link(dve.tensor_scalar(pb.bitcast(U32), posu, 15, None, ALU.bitwise_and))
                        link(dve.tensor_copy(paf[:, :, :], pa.bitcast(U32)))
                        link(dve.tensor_copy(pbf[:, :, :], pb.bitcast(U32)))
                        if t:
                            dve.wait_ge(*at("route", pp, 0))
                        i4 = i16f[:, :, :].rearrange("p (h q) k -> p h q k", q=2)
                        for q, pf in enumerate((paf, pbf)):
                            link(tt(eqm, over(pf.rearrange("p h k -> p (h k)"), TOPK), rep(iota[:, 0:TOPK], P),
                                    ALU.is_equal))
                            link(tt(prod.rearrange("p (h k) j -> p h k j", h=PH),
                                    eqm.rearrange("p (h k) j -> p h k j", h=PH),
                                    i4[:, :, q, :].unsqueeze(2).broadcast_to([P, PH, TOPK, TOPK]), ALU.mult))
                            link(dve.tensor_reduce(sel[:, q, :], prod, AX.X, ALU.add))
                        dve.wait_ge(*at("gate_x", pp, t))
                        link(dve.tensor_reduce(g8, sc16[:, :, :], AX.X, ALU.add))
                        link(dve.reciprocal(g8, g8))
                        tt(sel[:, 2, :].rearrange("p (h k) -> p h k", h=PH), sc16[:, :, :], over(g8, TOPK), ALU.mult
                           ).then_inc(*inc("sel", pp, t))
                    if pp == MOD_AHEAD:
                        modulation(l + 1)
                    dve.wait_ge(*at("route_read", pp, 1))
                    if upto < 6:
                        break
                    g0 = passes_before(pp) * (SEQ // 4)
                    with dve.Fori(0, SEQ // 8) as it:
                        for bf in range(2):
                            dve.wait_ge(cnt.sem("g_product"), it * 2 + (g0 + bf + 1))
                            for tt_ in range(4):
                                tk = it * 8 + (4 * bf + tt_)
                                dve.tensor_scalar(hot[:, bf, 0, tt_, :], iota, RT[:, 0, bass.ds(tk, 1)],
                                                  RT[:, 2, bass.ds(tk, 1)], ALU.is_equal, ALU.mult)
                            i = tt(hot[:, bf, 1, :, :], rep(iota, 4),
                                   RT[:, 1, bass.ds(it * 8 + 4 * bf, 4)].unsqueeze(2).broadcast_to([P, 4, P]),
                                   ALU.is_equal)
                            i.then_inc(cnt.sem("hot_ready"), 1)
                    c0 = passes_before(pp) * CHUNKS
                    dve.wait_ge(cnt.sem("g_bank_free"), g0 + 2 + SEQ // 4)
                    p = passes_before(pp)
                    dve.memset(wt[:, :, :, :].bitcast(F32), 0.0).then_inc(*inc("zeros", pp))
                    dve.wait_ge(*at("h2hi", pp))
                    tt(h2lo[:, :, :], h2T[:, :, :], h2hi[:, :, :].bitcast(F32), ALU.subtract).then_inc(*inc("h2lo", pp))
                    dve.wait_ge(*at("acc_clear", pp))
                    if p == 0:
                        dve.sem_inc(cnt.sem("ge_free"), 1)

                    def low(it, i_):
                        for hf in range(2):
                            dve.wait_ge(cnt.sem("high_made"), it * 8 + (p * 2 * N_ITEMS + 2 * i_ + hf + 1))
                            tt(halves[:, 2 * (i_ % 2) + hf, 1, :], raw[:, i_ % 4, hf * HALF:(hf + 1) * HALF],
                               halves[:, 2 * (i_ % 2) + hf, 0, :].bitcast(F32), ALU.subtract
                               ).then_inc(cnt.sem("low_made"), 1)

                    def weigh(it, c, par):
                        g = G[:, bass.ds(it * 2 + c, 1), :].rearrange("p a b -> p (a b)")
                        dve.wait_ge(cnt.sem("u_bank_free"), it * 2 + (p * CHUNKS + c + 3))
                        tt(g, ge, g, ALU.mult).then_inc(cnt.sem("ge_free"), 1)
                        dve.wait_ge(cnt.sem("ge_free"), it * 2 + (p * CHUNKS + c + 2))
                        dve.wait_ge(cnt.sem("half_free"), it * 8 + (p * 2 * N_ITEMS + 4 * c + 2))
                        dve.tensor_scalar(wt[:, par, 0, :], g, 1.0, None, ALU.mult).then_inc(cnt.sem("w_high"), 1)
                        dve.wait_ge(cnt.sem("w_high"), it * 2 + (p * CHUNKS + c + 1))
                        tt(wt[:, par, 1, :], g, wt[:, par, 0, :].bitcast(F32), ALU.subtract
                           ).then_inc(cnt.sem("w_ready"), 1)

                    low(0, 0)
                    low(0, 1)
                    weigh(0, 0, 0)
                    low(0, 2)
                    with dve.Fori(0, ITER) as it:
                        for c in (1, 2):
                            low(it, u_item(c + 1))
                            weigh(it, c, c % 2)
                            low(it, v_item(c))
                    weigh(0, CHUNKS - 1, 1)
                    low(0, N_ITEMS - 1)
                    dve.wait_ge(cnt.sem("half_free"), (p + 1) * 2 * N_ITEMS + 4)
                    for j in range(KB):
                        i = dve.scalar_tensor_tensor(out=XT[:, j, tok], in0=ps[j // 2][:, (j % 2) * SEQ:(j % 2 + 1) * SEQ],
                                                     scalar=mod[:, l, 40 + j, s_:s_ + 1], in1=XT[:, j, tok],
                                                     op0=ALU.mult, op1=ALU.add)
                    i.then_inc(*inc("x_moe", pp))
                    dve.wait_ge(*at("x_moe", pp))
        return cnt


def lay_out(inputs):
    f = {k: np.asarray(v) for k, v in inputs.items()}
    L = DEPTH

    def columns(a):
        return np.asarray(a).reshape(-1, P).T

    def slots(w, width=256):
        m = w.shape[2] // width
        return w.reshape(L, KB, P, m, width).transpose(0, 3, 2, 1, 4).reshape(L, m, P, KB * width)

    x = np.concatenate([f["ctx"][0], f["x"][0]], axis=0)
    x = x.reshape(T, KB, P).transpose(2, 1, 0)
    c = np.stack([columns(f["c_ctx"]), columns(f["c"][0])], axis=2)
    w = f["w_in"]
    names = ("aq", "ak", "av", "z", "xbc", "dt", "mq", "mk", "mv", "mo", "if", "gate")
    widths = (512, 128, 128, 512, 768, 16, 512, 512, 512, 512, 16, 3072)
    at_ = dict(zip(names, zip(np.cumsum((0,) + widths[:-1]), widths)))

    def part(name):
        a, n = at_[name]
        return w[:, :, a:a + n]

    aq = part("aq").reshape(L, D, 2, 4, AD).transpose(0, 1, 3, 2, 4).reshape(L, D, 512)
    xbc = part("xbc")
    gate = part("gate").reshape(L, D, 3, KB, P).transpose(0, 1, 3, 2, 4).reshape(L, D, 3072)
    win = np.concatenate([part("ak"), part("av"), xbc[:, :, 512:], xbc[:, :, :512], aq, part("mk"), part("mq"),
                          part("z"), part("mv"), part("mo"), gate], axis=2)
    wsm = np.concatenate([part("dt"), part("if")], axis=2).reshape(L, KB, P, 32).transpose(0, 2, 1, 3)
    wbr = f["w_branch"].reshape(L, 12, P, KB, P).transpose(0, 3, 2, 1, 4).reshape(L, KB, P, 1536)
    sub = f["peer_subkeys"].reshape(L, 16, KEYS, P).transpose(0, 3, 1, 2).reshape(L, P, SLOT)
    u = f["peer_u"].reshape(L, KEYS, CHUNKS, KB, P).transpose(0, 2, 4, 3, 1).reshape(L, CHUNKS, P, D)
    v = f["peer_v"].reshape(L, KEYS, CHUNKS, D).transpose(0, 2, 1, 3)
    vec = []
    for l in range(L):
        cw = f["ssd_conv_w"][l].reshape(TAPS, 6, P).transpose(2, 1, 0).reshape(P, 30)
        rows = np.concatenate([f["ssd_dt_bias"][l].ravel(), f["ml_gate_bias"][l].ravel(),
                               f["ssd_a_log"][l].ravel(), f["ssd_d"][l]])
        vec.append(np.concatenate([
            columns(f["norm1_g"][l]), columns(f["norm2_g"][l]), columns(f["b_mod"][l]), cw,
            columns(f["ssd_conv_b"][l]), columns(f["ssd_norm"][l]), columns(f["ml_norm"][l]),
            columns(np.tile(f["att_qnorm"][l], 2)), columns(np.tile(f["att_knorm"][l], 2)),
            np.broadcast_to(rows, (P, rows.size))], axis=1))
    vec = np.stack(vec, axis=1)
    assert vec.shape == (P, L, V_ALL)
    return {
        "x_in": x, "c_in": c, "wmod_in": slots(f["w_mod"]), "win_in": slots(win), "wsm_in": wsm, "wbr_in": wbr,
        "wout_in": slots(f["w_out"]), "wq_in": slots(f["peer_wq"]), "sub_in": sub, "u_in": u, "v_in": v,
        "vec_in": vec, "const_in": shape_constants(),
    }


def build_program(new_core, arrays, upto=99, limit=10**6):
    known = {}
    for _ in range(2):
        nc = new_core()
        args = [nc.dram_tensor(n, a.shape, F32, kind="ExternalInput").ap() for n, a in arrays.items()]
        out = nc.dram_tensor("out_0_dram", (P, KB, SEQ), F32, kind="ExternalOutput").ap()
        known = write_program(nc, *args, out, known, upto, limit).now
    return nc


def kernel(**inputs):
    import concourse.bacc as _bacc
    from concourse.bass_utils import run_bass_kernel_spmd as _run

    arrays = {n: np.ascontiguousarray(a) for n, a in lay_out(inputs).items()}
    nc = build_program(lambda: _bacc.Bacc("TRN2", target_bir_lowering=False, num_devices=1), arrays)
    r = _run(nc, [arrays], core_ids=[0])
    y = np.asarray(r.results[0]["out_0_dram"])
    return np.ascontiguousarray(y.transpose(2, 1, 0).reshape(1, SEQ, D))
```
